# Optimizing a Trainium2 kernel written in Bass

```python
import jax, jax.numpy as jnp
from jax import lax
import numpy as np

D_MODEL = 2048
BATCH = 1
SEQ = 256
DEPTH = 1

CTX_LEN = 256
GRID_W = 64
RET_HEADS = 8
RET_DK = 64
RET_DV = 128
RET_CHUNK = 128
ATT_HEADS = 16
ATT_KV_HEADS = 4
ATT_DH = 64
ATT_GROUP = ATT_HEADS // ATT_KV_HEADS
WINDOW = 128
ATT_BLOCK = 128
D_FF = -(-(8 * D_MODEL) // (3 * 256)) * 256
ROPE_BASE = 10000.0
NORM_EPS = 1e-6
PROJ_SIZES = (RET_HEADS * RET_DK, RET_HEADS * RET_DK, RET_HEADS * RET_DV, RET_HEADS * RET_DV,
              ATT_HEADS * ATT_DH, ATT_KV_HEADS * ATT_DH, ATT_KV_HEADS * ATT_DH)
D_PROJ = sum(PROJ_SIZES)
D_MIX_OUT = RET_HEADS * RET_DV + ATT_HEADS * ATT_DH

kernel_name = "hybrid_retention_window_gqa_dit_layer"

def _rmsnorm(x, g):
    xf = x.astype(jnp.float32)
    y = xf * lax.rsqrt(jnp.mean(xf * xf, axis=-1, keepdims=True) + NORM_EPS)
    return (y * g.astype(jnp.float32)).astype(x.dtype)

def _modulate(x, g, shift, scale):
    return _rmsnorm(x, g) * (1.0 + scale) + shift

def _split_proj(p):
    idx = [int(v) for v in np.cumsum(PROJ_SIZES)[:-1]]
    return jnp.split(p, idx, axis=-1)

def _heads(p, h, d):
    return p.reshape(p.shape[0], p.shape[1], h, d)

def _rope(x, pos):
    half = x.shape[-1] // 2
    inv = ROPE_BASE ** (-jnp.arange(half, dtype=jnp.float32) / half)
    ang = pos.astype(jnp.float32)[:, None] * inv[None, :]
    cos = jnp.cos(ang)[:, None, :]
    sin = jnp.sin(ang)[:, None, :]
    x1 = x[..., :half].astype(jnp.float32)
    x2 = x[..., half:].astype(jnp.float32)
    return jnp.concatenate([x1 * cos - x2 * sin, x1 * sin + x2 * cos], axis=-1).astype(x.dtype)

def _axial_rope(x, rows, cols):
    half = x.shape[-1] // 2
    return jnp.concatenate([_rope(x[..., :half], rows), _rope(x[..., half:], cols)], axis=-1)

def _ret_state(k, v, log_g):
    L = k.shape[1]
    w = jnp.exp(log_g[None, :] * (L - 1 - jnp.arange(L, dtype=jnp.float32))[:, None])
    return jnp.einsum('blhd,blhv->bhdv', k * w[None, :, :, None], v).astype(jnp.float32)

def _retention_chunkwise(q, k, v, log_g, s0, include_diag):
    b, L, h, dk = q.shape
    dv = v.shape[-1]
    C = RET_CHUNK
    n = L // C
    qc = q.reshape(b, n, C, h, dk)
    kc = k.reshape(b, n, C, h, dk)
    vc = v.reshape(b, n, C, h, dv)
    pos = jnp.arange(C, dtype=jnp.float32)
    rel = pos[:, None] - pos[None, :]
    mask = (rel >= 0) if include_diag else (rel > 0)
    decay_in = jnp.where(mask[None], jnp.exp(log_g[:, None, None] * jnp.maximum(rel, 0.0)[None]), 0.0)
    scores = jnp.einsum('bnihd,bnjhd->bnhij', qc, kc) * decay_in[None, None]
    o_in = jnp.einsum('bnhij,bnjhv->bnihv', scores, vc)
    k_w = jnp.exp(log_g[None, :] * (C - 1 - pos)[:, None])
    kv_chunk = jnp.einsum('bnjhd,bnjhv->nbhdv', kc * k_w[:, :, None], vc).astype(jnp.float32)
    g_chunk = jnp.exp(log_g * C)[None, :, None, None]

    def step(s, kv):
        return g_chunk * s + kv, s

    _, s_prev = lax.scan(step, s0.astype(jnp.float32), kv_chunk)
    q_w = jnp.exp(log_g[None, :] * (pos + 1.0)[:, None])
    o_x = jnp.einsum('bnihd,nbhdv->bnihv', qc * q_w[:, :, None], s_prev)
    return (o_in + o_x).reshape(b, L, h, dv)

def _bidir_retention(q, k, v, gate, lg_f, lg_b, s_f, s_b):
    o_f = _retention_chunkwise(q, k, v, lg_f, s_f, True)
    o_b = _retention_chunkwise(q[:, ::-1], k[:, ::-1], v[:, ::-1], lg_b, s_b, False)[:, ::-1]
    o = (o_f + o_b).astype(jnp.float32)
    o = o * lax.rsqrt(jnp.mean(o * o, axis=-1, keepdims=True) + NORM_EPS)
    o = o.reshape(o.shape[0], o.shape[1], RET_HEADS * RET_DV)
    return (o * jax.nn.silu(gate.astype(jnp.float32))).astype(gate.dtype)

def _window_attention(q, k, v, k_ctx, v_ctx, sink):
    b, L = q.shape[0], q.shape[1]
    Lc = k_ctx.shape[1]
    Bk = ATT_BLOCK
    n = L // Bk
    qb = q.reshape(b, n, Bk, ATT_KV_HEADS, ATT_GROUP, ATT_DH)
    pad = ((0, 0), (Bk, Bk), (0, 0), (0, 0))
    kp = jnp.pad(k, pad)
    vp = jnp.pad(v, pad)
    kb = jnp.concatenate([kp[:, j * Bk:j * Bk + L].reshape(b, n, Bk, ATT_KV_HEADS, ATT_DH) for j in range(3)], axis=2)
    vb = jnp.concatenate([vp[:, j * Bk:j * Bk + L].reshape(b, n, Bk, ATT_KV_HEADS, ATT_DH) for j in range(3)], axis=2)
    scale = ATT_DH ** -0.5
    s_loc = jnp.einsum('bnqkgd,bnskd->bnkgqs', qb, kb).astype(jnp.float32) * scale
    s_ctx = jnp.einsum('bnqkgd,bckd->bnkgqc', qb, k_ctx).astype(jnp.float32) * scale
    blk = jnp.arange(n)[:, None]
    qpos = (blk * Bk + jnp.arange(Bk)[None, :])[:, :, None]
    kpos = ((blk - 1) * Bk + jnp.arange(3 * Bk)[None, :])[:, None, :]
    valid = (jnp.abs(qpos - kpos) <= WINDOW) & (kpos >= 0) & (kpos < L)
    s_loc = jnp.where(valid[None, :, None, None], s_loc, -jnp.inf)
    sink_b = jnp.broadcast_to(sink.astype(jnp.float32).reshape(ATT_KV_HEADS, ATT_GROUP)[None, None, :, :, None, None],
                              s_loc.shape[:-1] + (1,))
    p = jax.nn.softmax(jnp.concatenate([s_loc, s_ctx, sink_b], axis=-1), axis=-1)
    p_loc = p[..., :3 * Bk].astype(v.dtype)
    p_ctx = p[..., 3 * Bk:3 * Bk + Lc].astype(v.dtype)
    o = jnp.einsum('bnkgqs,bnskd->bnqkgd', p_loc, vb) + jnp.einsum('bnkgqc,bckd->bnqkgd', p_ctx, v_ctx)
    return o.reshape(b, L, ATT_HEADS * ATT_DH)

def _context_attention(q, k, v, sink):
    b, Lc = q.shape[0], q.shape[1]
    qg = q.reshape(b, Lc, ATT_KV_HEADS, ATT_GROUP, ATT_DH)
    s = jnp.einsum('bqkgd,bckd->bkgqc', qg, k).astype(jnp.float32) * (ATT_DH ** -0.5)
    sink_b = jnp.broadcast_to(sink.astype(jnp.float32).reshape(ATT_KV_HEADS, ATT_GROUP)[None, :, :, None, None],
                              s.shape[:-1] + (1,))
    p = jax.nn.softmax(jnp.concatenate([s, sink_b], axis=-1), axis=-1)[..., :Lc].astype(v.dtype)
    o = jnp.einsum('bkgqc,bckd->bqkgd', p, v)
    return o.reshape(b, Lc, ATT_HEADS * ATT_DH)

def _swiglu(h, w_gate, w_up, w_down):
    return (jax.nn.silu(h @ w_gate) * (h @ w_up)) @ w_down

def setup_inputs(seed: int = 0) -> dict:
    key = jax.random.key(seed)
    ks = jax.random.split(key, 18)

    def nrm(k, shape, scale):
        return jax.random.normal(k, shape, jnp.float32) * scale

    base_decay = np.log(-np.log1p(-2.0 ** (-5.0 - np.arange(RET_HEADS)))).astype(np.float32)
    return {
        "x": nrm(ks[0], (BATCH, SEQ, D_MODEL), 1.0),
        "c": nrm(ks[1], (BATCH, D_MODEL), 1.0),
        "ctx": nrm(ks[2], (BATCH, CTX_LEN, D_MODEL), 1.0),
        "c_ctx": nrm(ks[3], (D_MODEL,), 1.0),
        "w_mod": nrm(ks[4], (DEPTH, D_MODEL, 6 * D_MODEL), 0.5 * D_MODEL ** -0.5),
        "b_mod": nrm(ks[5], (DEPTH, 6 * D_MODEL), 0.02),
        "norm_mix": 1.0 + nrm(ks[6], (DEPTH, D_MODEL), 0.02),
        "norm_ffn": 1.0 + nrm(ks[7], (DEPTH, D_MODEL), 0.02),
        "w_in": nrm(ks[8], (DEPTH, D_MODEL, D_PROJ), D_MODEL ** -0.5),
        "ret_decay": jnp.asarray(base_decay)[None, None, :] + nrm(ks[9], (DEPTH, 2, RET_HEADS), 0.05),
        "attn_sink": nrm(ks[10], (DEPTH, ATT_HEADS), 0.5),
        "w_out": nrm(ks[11], (DEPTH, D_MIX_OUT, D_MODEL), D_MIX_OUT ** -0.5),
        "w_gate": nrm(ks[12], (DEPTH, D_MODEL, D_FF), D_MODEL ** -0.5),
        "w_up": nrm(ks[13], (DEPTH, D_MODEL, D_FF), D_MODEL ** -0.5),
        "w_down": nrm(ks[14], (DEPTH, D_FF, D_MODEL), D_FF ** -0.5),
        "norm_final": 1.0 + nrm(ks[15], (D_MODEL,), 0.02),
    }

def reference(x, c, ctx, c_ctx, w_mod, b_mod, norm_mix, norm_ffn, w_in, ret_decay, attn_sink,
              w_out, w_gate, w_up, w_down, norm_final):
    L = x.shape[1]
    ROWS = L // GRID_W
    t = jnp.arange(L)
    rows = jnp.repeat(jnp.arange(ROWS), GRID_W)
    cols = jnp.tile(jnp.arange(GRID_W), ROWS)
    k_scale = RET_DK ** -0.5
    xc = ctx
    for l in range(DEPTH):
        last = l == DEPTH - 1
        mod = (jax.nn.silu(c) @ w_mod[l] + b_mod[l])[:, None, :]
        mod_c = (jax.nn.silu(c_ctx) @ w_mod[l] + b_mod[l])[None, None, :]
        sh_m, sc_m, gt_m, sh_f, sc_f, gt_f = jnp.split(mod, 6, axis=-1)
        sh_mc, sc_mc, gt_mc, sh_fc, sc_fc, gt_fc = jnp.split(mod_c, 6, axis=-1)
        lg_f = -jnp.exp(ret_decay[l, 0].astype(jnp.float32))
        lg_b = -jnp.exp(ret_decay[l, 1].astype(jnp.float32))

        hx = _modulate(x, norm_mix[l], sh_m, sc_m)
        hc = _modulate(xc, norm_mix[l], sh_mc, sc_mc)
        rq, rk, rv, rg, aq, ak, av = _split_proj(hx @ w_in[l])
        crq, crk, crv, crg, caq, cak, cav = _split_proj(hc @ w_in[l])

        crk = _heads(crk, RET_HEADS, RET_DK) * k_scale
        crv = _heads(crv, RET_HEADS, RET_DV)
        s_f = _ret_state(crk, crv, lg_f)
        s_b = _ret_state(crk[:, ::-1], crv[:, ::-1], lg_b)
        q_r = _rope(_heads(rq, RET_HEADS, RET_DK), t)
        k_r = _rope(_heads(rk, RET_HEADS, RET_DK), t) * k_scale
        v_r = _heads(rv, RET_HEADS, RET_DV)
        y_ret = _bidir_retention(q_r, k_r, v_r, rg, lg_f, lg_b, s_f, s_b)

        cak = _heads(cak, ATT_KV_HEADS, ATT_DH)
        cav = _heads(cav, ATT_KV_HEADS, ATT_DH)
        q_a = _axial_rope(_heads(aq, ATT_HEADS, ATT_DH), rows, cols)
        k_a = _axial_rope(_heads(ak, ATT_KV_HEADS, ATT_DH), rows, cols)
        v_a = _heads(av, ATT_KV_HEADS, ATT_DH)
        y_att = _window_attention(q_a, k_a, v_a, cak, cav, attn_sink[l])

        x = x + gt_m * (jnp.concatenate([y_ret, y_att], axis=-1) @ w_out[l])

        if not last:
            zero = jnp.zeros((xc.shape[0], RET_HEADS, RET_DK, RET_DV), jnp.float32)
            y_ret_c = _bidir_retention(_heads(crq, RET_HEADS, RET_DK), crk, crv, crg, lg_f, lg_b, zero, zero)
            y_att_c = _context_attention(_heads(caq, ATT_HEADS, ATT_DH), cak, cav, attn_sink[l])
            xc = xc + gt_mc * (jnp.concatenate([y_ret_c, y_att_c], axis=-1) @ w_out[l])
            xc = xc + gt_fc * _swiglu(_modulate(xc, norm_ffn[l], sh_fc, sc_fc), w_gate[l], w_up[l], w_down[l])

        x = x + gt_f * _swiglu(_modulate(x, norm_ffn[l], sh_f, sc_f), w_gate[l], w_up[l], w_down[l])
    return _rmsnorm(x, norm_final)


_drawn_inputs = setup_inputs


def setup_inputs(seed=0):
    import zlib

    import numpy as np

    out = dict(_drawn_inputs(seed))
    spreads = {}
    factors = {'norm_mix': 8.0, 'norm_ffn': 8.0, 'attn_sink': 8.0, 'norm_final': 2.743}
    for name, (base, spread) in spreads.items():
        noise = np.random.default_rng([zlib.crc32(name.encode()), seed]).standard_normal(out[name].shape)
        drawn = base * np.exp(spread * noise) if base else spread * noise
        out[name] = __import__('jax').numpy.asarray(drawn.astype(out[name].dtype))
    for name, factor in factors.items():
        out[name] = (out[name] * factor).astype(out[name].dtype)
    return out
```

```python
import concourse.bass as bass
from concourse import mybir
from contextlib import ExitStack

P = 128
SEQ, CTX, D = 256, 256, 2048
KT = D // P
TT = SEQ // P
RH, RDK, RDV = 8, 64, 128
AH, KVH, DH = 16, 4, 64
DFF = 5632
FG = DFF // 512
CW = 512
RAW, SPLIT, LEAD = 8, 4, 4
CT = KT // 2
EPS = 1e-6
SCALE = DH ** -0.5

N_MOD = 0
N_IN = N_MOD + 4 * KT
N_OUT = N_IN + 9 * CT
N_GU = N_OUT + 4 * CT
N_DN = N_GU + 2 * FG * CT
N_END = N_DN + FG * CT

CA = {}
CB = {}
_at = 0
for _n, _w in (("ident", P), ("ones", P), ("mask", 2 * P), ("rq_cos", 64), ("rq_sin", 64), ("rk_cos", 64),
               ("rk_sin", 64), ("ax_cos", 64), ("ax_sin", 64), ("expo", 4), ("sel", 2)):
    CA[_n] = (_at, _at + _w)
    _at += _w
NCA = _at
_at = 0
for _n, _w in (("ahead", 512), ("behind", 512), ("pos_f", 256), ("pos_b", 256)):
    CB[_n] = (_at, _at + _w)
    _at += _w
NCB = _at


def build(nc, x, c, ctx, c_ctx, w_mod, b_mod, norm_mix, norm_ffn, w_in, ret_decay, attn_sink,
          w_out, w_gate, w_up, w_down, norm_final, const_a, const_b, out):
    f32, f32r = mybir.dt.float32, mybir.dt.float32r
    ACT, ALU, AX = mybir.ActivationFunctionType, mybir.AluOpType, mybir.AxisListType
    ds = bass.ds
    stack = ExitStack()
    with stack:
        base = (nc.sbuf_base + 63) // 64 * 64
        at = [base]

        def place(name, shape, dt=f32, offset=None):
            size = 4
            for n in shape[1:]:
                size *= n
            if offset is None:
                offset = at[0]
                at[0] += (size + 31) // 32 * 32
            assert offset + size <= nc.sbuf_usable_end, name
            return nc.alloc_sbuf_tensor_at(name, shape, dt, offset=offset)

        K1 = 1024
        ca = place("const_a_sb", [P, NCA])
        cb_at = at[0]
        cb = place("const_b_sb", [P, NCB])
        h_at = at[0]
        h_hi = place("h_hi", [P, KT, SEQ], f32r)
        h_lo = place("h_lo", [P, KT, SEQ], f32r)
        px_at = at[0]
        proj_x = place("proj_x", [P, 4, TT, CW])
        ch_at = at[0]
        c_hi = place("c_hi", [P, KT, CTX], f32r)
        c_lo = place("c_lo", [P, KT, CTX], f32r)
        pc_at = at[0]
        proj_c = place("proj_c", [P, 4, TT, CW])
        raw = [place(f"raw{s}", [P, 1024]) for s in range(RAW)]
        w_hi = [place(f"w_hi{s}", [P, 1024], f32r) for s in range(SPLIT)]
        w_lo = [place(f"w_lo{s}", [P, 1024], f32r) for s in range(SPLIT)]
        m_at = at[0]
        mraw = [place(f"mraw{s}", [P, 1024]) for s in range(2)]
        acc_at = at[0]
        acc = place("acc", [P, 3 * D])
        rows_a = place("rows_a", [P, P])
        rows_b = place("rows_b", [2 * KT, P])
        vec_t = place("vec_t", [P, P])
        s32 = place("s32", [P, 2 * KT])
        c4 = place("c4", [P, KT, 2, 2], f32r)
        modc = place("modc", [P, 2 * KT, 2])
        gm = place("gm", [P, KT, 2])
        stat = place("stat", [P, 4, 4])
        lg_raw = place("lg_raw", [P, 2, RH])
        lg_e = place("lg_e", [P, 2, RH])
        lg_n = place("lg_n", [P, 2, RH])
        lg_p = place("lg_p", [P, 2, RH // 2])
        sink = place("sink", [P, AH])
        nsink = place("nsink", [P, AH])
        wexp = place("wexp", [P, TT, 2, RH])
        wck = place("wck", [P, TT, 2, RH])
        rmax = place("rmax", [P, 32])
        nmax = place("nmax", [P, 32])
        rsum = place("rsum", [P, 32])
        sinkm = place("sinkm", [P, 32])
        sinke = place("sinke", [P, 32])
        den = place("den", [P, 32])
        rden = place("rden", [P, 32])
        rss = place("rss", [P, 4, 16])
        sh_f = place("sh_f", [P, KT])
        gm_f = place("gm_f", [P, KT])
        ss_d = place("ss_d", [P, TT, 4])
        st_d = place("st_d", [P, 4, TT])
        ss_f = place("ss_f", [P, TT, 4])
        st_f = place("st_f", [P, 4, TT])

        xin = place("xin", [P, 4, D], offset=h_at)
        xt_x = place("xt_x", [P, KT, SEQ], offset=px_at)
        xt_c = place("xt_c", [P, KT, CTX], offset=pc_at)
        mod_rows = place("mod_rows", [4, 2 * D], offset=ch_at)
        junk0 = place("junk0", [P, D], offset=m_at)
        tmp_s = place("tmp_s", [P, 4, 2, 256], offset=m_at)
        proj_y = place("proj_y", [P, 5, TT, CW], offset=ch_at)
        rope_t = place("rope_t", [P, 4, 256], offset=ch_at + 20 * K1)
        ckw = place("ckw", [P, TT, 2, RH, RDK], offset=ch_at + 24 * K1)
        qk_t = place("qk_t", [P, 4, 2, SEQ], offset=h_at)
        aq_t = place("aq_t", [P, 8, SEQ], offset=h_at + 8 * K1)
        ak_t = place("ak_t", [P, KVH // 2, SEQ + CTX], offset=h_at + 16 * K1)
        darg = [place(f"darg{s}", [P, 512], offset=h_at + (24 + 2 * s) * K1) for s in range(2)]
        qw = [place(f"qw{s}", [P, 2, SEQ], offset=h_at + (28 + 2 * s) * K1) for s in range(2)]
        dec = [place(f"dec{s}", [P, 512], offset=px_at + 2 * s * K1) for s in range(2)]
        rp = [place(f"rp{s}", [P, 2, SEQ], offset=pc_at + 2 * s * K1) for s in range(2)]
        wtab = [place(f"wtab{s}", [P, 2, SEQ], offset=ch_at + 2 * s * K1) for s in range(2)]
        s_sb = [place(f"s_sb{s}", [P, 2, RDV], offset=ch_at + (20 + s) * K1) for s in range(2)]
        pt = [place(f"pt{s}", [P, 4, P], offset=h_at + (24 + 2 * s) * K1) for s in range(2)]
        prob = [place("prob0", [P, 512], offset=h_at + 20 * K1), place("prob1", [P, 512], offset=h_at + 22 * K1),
                place("prob2", [P, 512], offset=ch_at + 22 * K1)]
        dexp = [place(f"dexp{s}", [P, 512], offset=m_at + 2 * s * K1) for s in range(2)]
        junk1 = place("junk1", [P, 2, P], offset=m_at + 4 * K1)
        xr = place("xr", [P, TT, D], offset=px_at)
        tmp_d = place("tmp_d", [P, TT, CW], offset=pc_at)
        junk2 = place("junk2", [P, TT, CW], offset=pc_at + 4 * K1)
        xn = place("xn", [P, TT, D], offset=ch_at)
        tmp_e = place("tmp_e", [P, 4, 256], offset=pc_at + 8 * K1)
        act_t = place("act_t", [P, 4 * FG, SEQ], offset=ch_at)
        act = place("act", [P, TT, CW], offset=ch_at + 44 * K1)
        sg = place("sg", [P, TT, CW], offset=cb_at)
        st_hi = [place(f"st_hi{s}", [P, 4, SEQ], f32r, offset=acc_at + 4 * s * K1) for s in range(2)]
        st_lo = [place(f"st_lo{s}", [P, 4, SEQ], f32r, offset=acc_at + (16 + 4 * s) * K1) for s in range(2)]
        nf = place("nf", [P, D], offset=h_at)
        tmp_f = place("tmp_f", [P, TT, CW], offset=h_at + 8 * K1)
        junk3 = place("junk3", [P, CW], offset=h_at + 12 * K1)

        ps = stack.enter_context(nc.psum_tensor("ps", [P, 8 * CW], f32))

        def bank(b, lo=0, hi=CW):
            return ps[:, b * CW + lo:b * CW + hi]

        def A(name, lo=0, hi=None):
            s, e = CA[name]
            return ca[:, s + lo:(s + hi if hi is not None else e)]

        def Bc(name):
            s, e = CB[name]
            return cb[:, s:e]

        ident = A("ident")

        def spread(ap, axis, n):
            ap = ap.unsqueeze(axis)
            shape = list(ap.shape)
            shape[axis] = n
            return ap.to_broadcast(shape)

        def sem(name):
            return stack.enter_context(nc.semaphore(name))

        raw_in = [sem(f"raw_in{s}") for s in range(RAW)]
        hi_done = sem("hi_done")
        lo_done = sem("lo_done")
        used = sem("used")
        mraw_in = [sem(f"mraw_in{s}") for s in range(2)]
        acc_step = sem("acc_step")
        in_rows, in_small, in_ca, in_cb = sem("in_rows"), sem("in_small"), sem("in_ca"), sem("in_cb")
        in_x = [sem(f"in_x{t}") for t in range(4)]
        vec_tr, vec_cp, silu_c, c4_hi, c4_lo = sem("vec_tr"), sem("vec_cp"), sem("silu_c"), sem("c4_hi"), sem("c4_lo")
        sq_done, ms_done, sd_done, rs_done, xn_done = sem("sq_done"), sem("ms_done"), sem("sd_done"), sem("rs_done"), sem("xn_done")
        xt_done, xt_a, xt_d = sem("xt_done"), sem("xt_a"), sem("xt_d")
        rows_done, cols_done, modc_done, gm_done = sem("rows_done"), sem("cols_done"), sem("modc_done"), sem("gm_done")
        hm_done, hh_done, hl_done = sem("hm_done"), sem("hh_done"), sem("hl_done")
        proj_out = sem("proj_out")
        acc_bias, ckw_done, gb_d = sem("acc_bias"), sem("ckw_done"), sem("gb_d")
        lg_done, pool_step, rope_done, wck_done = sem("lg_done"), sem("pool_step"), sem("rope_done"), sem("wck_done")
        wexp_done, small_prep = sem("wexp_done"), sem("small_prep")
        bt_done, bt_a, bt_d = sem("bt_done"), sem("bt_a"), sem("bt_d")
        gb_done, gb_a, shc_done, shf_done = sem("gb_done"), sem("gb_a"), sem("shc_done"), sem("shf_done")
        dexp_done, darg_done, dec_done, wtab_done, qw_done = sem("dexp_done"), sem("darg_done"), sem("dec_done"), sem("wtab_done"), sem("qw_done")
        st_mm, st_cp, rsc_mm, rp_done, ro_mm, ro_sq, ro_out = (sem(n) for n in (
            "st_mm", "st_cp", "rsc_mm", "rp_done", "ro_mm", "ro_sq", "ro_out"))
        sc_mm, mx_done, nm_done, ex_done, pt_mm, pt_a, pt_d, pv_mm, sk_m, sk_e, dn_done, rd_done, ya_done = (sem(n) for n in (
            "sc_mm", "mx_done", "nm_done", "ex_done", "pt_mm", "pt_a", "pt_d", "pv_mm", "sk_m", "sk_e", "dn_done", "rd_done", "ya_done"))
        rr_m, rr_s, rr_r, yr_done = sem("rr_m"), sem("rr_s"), sem("rr_r"), sem("yr_done")
        yt_mm, yt_hi, yt_lo = sem("yt_mm"), sem("yt_hi"), sem("yt_lo")
        in_xr, d_scaled, d_out, d_sq = sem("in_xr"), sem("d_scaled"), sem("d_out"), sem("d_sq")
        dm_done, dsd_done, drs_done, xn2_done = sem("dm_done"), sem("dsd_done"), sem("drs_done"), sem("xn2_done")
        scc_done, gmf_done, et_mm, em_done, eh_done, el_done = (sem(n) for n in (
            "scc_done", "gmf_done", "et_mm", "em_done", "eh_done", "el_done"))
        sg_done, act_done, at_mm, at_out = sem("sg_done"), sem("act_done"), sem("at_mm"), sem("at_out")
        acc_zero2, acc_bias2, gf_mm, gf_a, gf_d = sem("acc_zero2"), sem("acc_bias2"), sem("gf_mm"), sem("gf_a"), sem("gf_d")
        sth_done, stl_done = sem("sth_done"), sem("stl_done")
        in_nf, f_scaled, f_out, f_sq, fm_done, fsd_done, frs_done, fin_done, stored = (sem(n) for n in (
            "in_nf", "f_scaled", "f_out", "f_sq", "fm_done", "fsd_done", "frs_done", "fin_done", "stored"))

        A0 = 4
        GATE_M = 0
        SHIFT_F, SCALE_F, GATE_F = D, 2 * D, D

        BT_BANKS = (2, 3, 6, 7)

        def mix_dst(g):
            if g < 4:
                return qk_t[:, g, :, :].rearrange("p a c -> p (a c)")
            if g < 8:
                return aq_t[:, 2 * (g - 4):2 * (g - 4) + 2, :].rearrange("p a c -> p (a c)")
            return ak_t[:, g - 8, :]

        def mix_evac(e, copy, parity, done):
            for g in range(parity, 10, 2):
                e.wait_ge(bt_done, g + 1)
                copy(mix_dst(g), bank(BT_BANKS[g % 4])).then_inc(done, 1)


        block = stack.enter_context(nc.Block())

        @block.sync
        def _(sp):
            def load(n, slot, src, wait=True):
                if wait:
                    sp.wait_ge(lo_done, n - (RAW - 1))
                dst = raw[slot][:, :]
                if len(src.shape) == 3:
                    dst = dst.rearrange("p (k c) -> p k c", k=2)
                sp.dma_start(dst, src).then_inc(raw_in[slot], 16)

            def half(w, row, col):
                return w[0, ds(row, 2 * P), ds(col, CW)].rearrange("(k p) c -> p k c", p=P)

            def mod_load(m, slot, kk, col):
                sp.wait_ge(acc_step, A0 - 2 + 2 * m if isinstance(m, int) else m * 2 + (A0 - 2))
                sp.dma_start(mraw[slot][:, :].rearrange("p (k c) -> p k c", k=2),
                             half(w_mod, kk * 2 * P, 2 * D + col)).then_inc(mraw_in[slot], 16)

            def mod_tile(q, k):
                return w_mod[0, k * P:(k + 1) * P, ds(q * 1024, 1024)]

            for n in range(KT):
                load(n, n % RAW, mod_tile(0, n), wait=n >= RAW)
            with sp.Fori(1, 4) as q:
                for t in range(KT):
                    load(q * KT + t, t % RAW, mod_tile(q, t))

            for t in range(CT):
                load(N_IN + t, t, half(w_in, 2 * t * P, CW))
            sp.wait_ge(hl_done, 2 * KT)
            with sp.Fori(0, 2) as i:
                for j, col in ((0, (i * 6 + 2) * CW), (1, (i * -3 + 3) * CW)):
                    for t in range(CT):
                        load(i * 16 + (N_IN + CT * (j + 1) + t), t, half(w_in, 2 * t * P, col))
                        for u in (2 * t, 2 * t + 1):
                            mod_load(i * 32 + (16 * j + u), u % 2, u % 8, i * (4 * CW) + (2 * j + u // 8) * CW)
            for j, (col, cc) in enumerate(((6, None), (7, 8), (4, None), (5, 9), (None, None))):
                for t in range(CT):
                    n = N_IN + CT * (5 + j) + t
                    if col is None:
                        load(n, t, half(w_out, (8 + 2 * t) % 16 * P, 0))
                    else:
                        load(n, t, half(w_in, 2 * t * P, col * CW))
                    if cc is not None:
                        mod_load(8 * cc + t, t % 2, t, cc * CW)

            sp.wait_ge(pv_mm, 32)
            sp.wait_ge(ro_mm, RH)
            sp.dma_start(xr[:, :, :], x[0].rearrange("(t p) d -> p t d", p=P)).then_inc(in_xr, 16)
            for j in range(4):
                for t in range(CT):
                    n = N_OUT + CT * (j + 1) + t
                    if j < 3:
                        load(n, t, half(w_out, (8 + 2 * t) % 16 * P, (j + 1) * CW))
                    else:
                        load(n, t, half(w_gate, 2 * t * P, 0))
                    if j in (0, 2):
                        cc = 10 + j // 2
                        mod_load(8 * cc + t, t % 2, t, cc * CW)

            def ffn_up(i, mods, last=False):
                for t in range(CT):
                    load(i * 16 + (N_GU + CT + t), t, half(w_up, 2 * t * P, i * CW))
                    if mods and t % 2 == 0:
                        u = t // 2
                        mod_load(i * 4 + (96 - 4 + u), u % 2, i - 1, 3 * D + u * CW)
                for t in range(CT):
                    if last:
                        load(N_DN + t, t, half(w_down, t % 2 * 2 * P, t // 2 * CW))
                    else:
                        load(i * 16 + (N_GU + 2 * CT + t), t, half(w_gate, 2 * t * P, i * CW + CW))

            ffn_up(0, False)
            sp.wait_ge(acc_bias2, 16)
            with sp.Fori(1, 9) as i:
                ffn_up(i, True)
            ffn_up(9, False)
            ffn_up(10, False, last=True)

            with sp.Fori(1, FG) as g:
                for t in range(CT):
                    load(g * CT + (N_DN + t), t, half(w_down, g * (4 * P) + t % 2 * 2 * P, t // 2 * CW))
            o = out[0].rearrange("(t p) d -> p t d", p=P)
            for t in range(TT):
                sp.wait_ge(fin_done, t + 1)
                sp.dma_start(o[:, t, :], xr[:, t, :]).then_inc(stored, 16)
            sp.wait_ge(stored, 16 * TT)

        @block.gpsimd
        def _(pool):
            steps = [0]

            def step(ins):
                steps[0] += 1
                ins.then_inc(pool_step, 1)

            def settle():
                pool.wait_ge(pool_step, steps[0])

            for r in range(A0):
                part = slice(r * 3 * D // A0, (r + 1) * 3 * D // A0)
                pool.memset(acc[:, part], 0.0).then_inc(acc_step, 1)
            pool.wait_ge(acc_step, A0)
            pool.dma_start(acc[0:1, :], b_mod[:, 2 * D:5 * D]).then_inc(acc_bias, 16)
            pool.wait_ge(lg_done, 1)
            step(pool.tensor_scalar(lg_n[:, :, :], lg_e[:, :, :], -1.0, None, ALU.mult))
            pool.wait_ge(in_small, 32)
            pool.tensor_scalar(nsink[:, :], sink[:, :], -1.0, None, ALU.mult).then_inc(small_prep, 1)
            settle()
            pairs = lg_n[:, :, :].rearrange("p d (h e) -> p d h e", e=2)
            for e in range(2):
                q = slice(64 * e, 64 * e + 64)
                pool.wait_ge(small_prep, 1 + e)
                pool.tensor_copy(lg_p[q, :, :], pairs[q, :, :, e]).then_inc(small_prep, 1)
            pool.wait_ge(small_prep, 3)
            pool.wait_ge(in_ca, 16)
            for lt in range(TT):
                for d in range(2):
                    pool.tensor_scalar(wexp[:, lt, d, :], lg_n[:, d, :], A("expo", 2 * lt + d, 2 * lt + d + 1), None,
                                       ALU.mult).then_inc(wexp_done, 1)

            turned = [0]

            def rope(v, cos, sin):
                for t in range(TT):
                    (a, b), cs, sn = v(t), cos(t), sin(t)
                    size = 1
                    for n in a.shape[1:]:
                        size *= n
                    tm = [rope_t[:, r, 0:size] for r in range(4)]
                    if len(a.shape) == 4:
                        tm = [r.rearrange("p (h a c) -> p h a c", a=a.shape[2], c=a.shape[3]) for r in tm]
                    else:
                        tm = [r.rearrange("p (h c) -> p h c", c=a.shape[2]) for r in tm]
                    step(pool.tensor_tensor(tm[0], a, cs, ALU.mult))
                    step(pool.tensor_tensor(tm[1], b, sn, ALU.mult))
                    step(pool.tensor_tensor(tm[2], a, sn, ALU.mult))
                    step(pool.tensor_tensor(tm[3], b, cs, ALU.mult))
                    settle()
                    pool.tensor_tensor(a, tm[0], tm[1], ALU.subtract).then_inc(rope_done, 1)
                    pool.tensor_tensor(b, tm[2], tm[3], ALU.add).then_inc(rope_done, 1)
                    turned[0] += 2
                    pool.wait_ge(rope_done, turned[0])

            def ret_half(src):
                def v(t):
                    w = src(t).rearrange("p (h c) -> p h c", c=RDK)
                    return w[:, :, 0:32], w[:, :, 32:64]
                return v

            def ax_half(src):
                def v(t):
                    w = src(t).rearrange("p (h a c) -> p h a c", a=2, c=32)
                    return w[:, :, :, 0:16], w[:, :, :, 16:32]
                return v

            def ret_tab(name):
                return lambda t: spread(A(name, 32 * t, 32 * t + 32), 1, RH)

            def ax_tab(name, heads):
                return lambda t: spread(A(name, 32 * t, 32 * t + 32).rearrange("p (a c) -> p a c", a=2), 1, heads)

            pool.wait_ge(proj_out, 5)
            rope(ret_half(lambda t: proj_x[:, 0, t, :]), ret_tab("rk_cos"), ret_tab("rk_sin"))
            pool.wait_ge(wck_done, 1)
            for lt in range(TT):
                for d in range(2):
                    pool.tensor_tensor(ckw[:, lt, d, :, :], proj_c[:, 0, lt, :].rearrange("p (h c) -> p h c", c=RDK),
                                       spread(wck[:, lt, d, :], 2, RDK), ALU.mult).then_inc(ckw_done, 1)
            rope(ax_half(lambda t: proj_x[:, 3, t, 0:256]), ax_tab("ax_cos", KVH), ax_tab("ax_sin", KVH))
            pool.wait_ge(proj_out, 6)
            rope(ret_half(lambda t: proj_y[:, 0, t, :]), ret_tab("rq_cos"), ret_tab("rq_sin"))
            for s in (1, 2):
                pool.wait_ge(proj_out, 6 + s)
                rope(ax_half(lambda t, s=s: proj_y[:, s, t, :]), ax_tab("ax_cos", 8), ax_tab("ax_sin", 8))
            pool.wait_ge(acc_step, A0 + 2 * 80)
            pool.wait_ge(in_cb, 16)
            for h in range(RH):
                if h >= 2:
                    pool.wait_ge(darg_done, h - 1)
                pool.tensor_scalar(dexp[h % 2][:, :], Bc("behind"), lg_n[:, 1, h:h + 1], None, ALU.mult).then_inc(dexp_done, 1)
            pool.wait_ge(shf_done, 1)
            pool.memset(acc[:, GATE_F:GATE_F + D], 0.0).then_inc(acc_zero2, 1)
            pool.wait_ge(acc_zero2, 1)
            pool.dma_start(acc[0:1, GATE_F:GATE_F + D], b_mod[:, 5 * D:6 * D]).then_inc(acc_bias2, 16)

        @block.scalar
        def _(act_e):
            e = act_e

            def hi(t, landed, freed):
                e.wait_ge(raw_in[t % RAW], landed)
                if freed is not None:
                    e.wait_ge(used, freed)
                e.activation(w_hi[t % SPLIT][:, :], raw[t % RAW][:, :], ACT.Copy).then_inc(hi_done, 1)

            def his(first, i, per, count):
                for t in range(LEAD, LEAD + count):
                    hi(t, i * (16 * per // RAW) + ((first + t) // RAW + 1) * 16, i * per + (first + t - (SPLIT - 1)))

            e.dma_start(rows_b[0:KT, :], c.rearrange("b (k p) -> (b k) p", p=P)).then_inc(in_rows, 16)
            e.dma_start(rows_b[KT:2 * KT, :], c_ctx.rearrange("(k p) -> k p", p=P)).then_inc(in_rows, 16)
            e.dma_start(ca[:, :], const_a).then_inc(in_ca, 16)
            e.dma_start(rows_a[0:96, :], b_mod.rearrange("b (k p) -> (b k) p", p=P)).then_inc(in_rows, 16)
            e.dma_start(rows_a[96:112, :], norm_mix.rearrange("b (k p) -> (b k) p", p=P)).then_inc(in_rows, 16)
            e.dma_start(rows_a[112:128, :], norm_ffn.rearrange("b (k p) -> (b k) p", p=P)).then_inc(in_rows, 16)
            e.dma_start(lg_raw[:, :, :].rearrange("p d h -> p (d h)"),
                        ret_decay.rearrange("b d h -> b (d h)")[0].partition_broadcast(P)).then_inc(in_small, 16)
            e.dma_start(sink[:, :], attn_sink[0].partition_broadcast(P)).then_inc(in_small, 16)
            for t in range(4):
                src = (x if t < 2 else ctx)[0, t % 2 * P:(t % 2 + 1) * P, :]
                e.dma_start(xin[:, t, :], src).then_inc(in_x[t], 16)
            e.dma_start(cb[:, :], const_b).then_inc(in_cb, 16)

            e.wait_ge(vec_tr, 2)
            e.activation(s32[:, :], bank(3, 0, 2 * KT), ACT.Silu).then_inc(silu_c, 1)
            e.wait_ge(silu_c, 1)
            e.activation(c4[:, :, :, 0], s32[:, :].rearrange("p (v k) -> p k v", v=2), ACT.Copy).then_inc(c4_hi, 1)
            for t in range(4):
                e.wait_ge(in_x[t], 16)
                if t:
                    e.wait_ge(sq_done, t)
                e.activation(junk0[:, :], xin[:, t, :], ACT.Square, accum_out=stat[:, 0, t:t + 1]).then_inc(sq_done, 1)
            e.wait_ge(ms_done, 1)
            e.activation(stat[:, 2, :], stat[:, 1, :], ACT.Sqrt).then_inc(sd_done, 1)
            e.wait_ge(in_small, 32)
            e.activation(lg_e[:, :, :], lg_raw[:, :, :], ACT.Exp).then_inc(lg_done, 1)
            for g in range(0, 16, 2):
                e.wait_ge(xt_done, g + 1)
                dst = (xt_x if g < 8 else xt_c)[:, g % 4 * 4:g % 4 * 4 + 4, g // 4 % 2 * P:(g // 4 % 2 + 1) * P]
                e.activation(dst, bank(4 + g % 4).rearrange("p (k c) -> p k c", k=4), ACT.Copy).then_inc(xt_a, 1)

            e.sem_inc(rows_done, 1)
            e.sem_inc(proj_out, 1)
            e.sem_inc(at_out, 1)
            for n in range(LEAD):
                hi(n, 16, None)
            with e.Fori(0, 2) as i:
                for j in range(2):
                    his(N_MOD + KT * j, i, 2 * KT, KT)
                    e.wait_ge(used, i * (2 * KT) + KT * (j + 1))
                    e.activation(mod_rows[:, ds(i * 2048 + j * 1024, 1024)], ps[0:4, j * 1024:(j + 1) * 1024], ACT.Copy).then_inc(rows_done, 1)
            with e.Fori(0, 4) as kq:
                for j in range(4):
                    e.wait_ge(hm_done, kq * 8 + 2 * j + 2)
                    e.activation(h_hi[:, ds(kq * 4 + j, 1), :].rearrange("p k c -> p (k c)"), tmp_s[:, j, 0, :], ACT.Copy).then_inc(hh_done, 1)
                    e.activation(c_hi[:, ds(kq * 4 + j, 1), :].rearrange("p k c -> p (k c)"), tmp_s[:, j, 1, :], ACT.Copy).then_inc(hh_done, 1)

            with e.Fori(0, 2) as i:
                for j in range(2):
                    his(N_IN + CT * j, i, 2 * CT, CT)
                    e.wait_ge(used, i * 16 + (N_IN + CT * (j + 1)))
                    e.activation(proj_x[:, ds(i * 2 + j, 1), :, :].rearrange("p s t c -> p (s t c)"),
                                 ps[:, j * 2048:j * 2048 + 1024], ACT.Copy)
                    e.activation(proj_c[:, ds(i * 2 + j, 1), :, :].rearrange("p s t c -> p (s t c)"),
                                 ps[:, j * 2048 + 1024:j * 2048 + 2048], ACT.Copy).then_inc(proj_out, 1)
            for s in range(5):
                his(N_IN + CT * (4 + s), 0, 0, CT)
                if s == 0:
                    e.wait_ge(wexp_done, 4)
                    e.activation(wck[:, :, :, :], wexp[:, :, :, :], ACT.Exp).then_inc(wck_done, 1)
                e.wait_ge(used, N_IN + CT * (5 + s))
                src = ps[:, s % 2 * 2048:s % 2 * 2048 + 1024]
                if s in (1, 2):
                    for t in range(TT):
                        ins = e.activation(proj_y[:, s, t, :].rearrange("p (h g c) -> p g h c", h=4, g=2),
                                           src[:, t * CW:(t + 1) * CW].rearrange("p (g h c) -> p g h c", g=2, h=4), ACT.Copy)
                else:
                    ins = e.activation(proj_y[:, s, :, :].rearrange("p t c -> p (t c)"), src, ACT.Silu if s >= 3 else ACT.Copy)
                ins.then_inc(proj_out, 1)

            mix_evac(e, lambda dst, src: e.activation(dst, src, ACT.Copy), 0, bt_a)
            for n in (0, 1):
                e.wait_ge(gb_done, n + 1)
                e.activation(acc[:, GATE_M + n * CW:GATE_M + (n + 1) * CW], bank((0, 1, 4, 5)[n]), ACT.Copy).then_inc(gb_a, 1)

            def decay(h):
                e.wait_ge(darg_done, h + 1)
                if h >= 2:
                    e.wait_ge(rp_done, h - 1)
                e.activation(dec[h % 2][:, :], darg[h % 2][:, :], ACT.Exp).then_inc(dec_done, 1)

            def weights(p):
                if p >= 2:
                    e.wait_ge(qw_done, p - 1)
                for d, name in enumerate(("pos_f", "pos_b")):
                    ins = e.activation(wtab[p % 2][:, d, :], Bc(name), ACT.Exp, scale=lg_p[:, d, p:p + 1])
                ins.then_inc(wtab_done, 1)

            def states(p):
                e.wait_ge(st_mm, p + 1)
                if p >= 2:
                    e.wait_ge(ro_mm, 2 * (p - 1))
                e.activation(s_sb[p % 2][:, :, :].rearrange("p d c -> p (d c)"), bank(0, 0, 256), ACT.Copy).then_inc(st_cp, 1)

            def probabilities(u):
                e.wait_ge(nm_done, u + 1)
                if u >= 3:
                    e.wait_ge(pt_mm, u - 2)
                e.activation(prob[u % 3][:, :], bank((3, 6, 7)[u % 3]), ACT.Exp, bias=nmax[:, u:u + 1], scale=SCALE,
                             accum_out=rsum[:, u:u + 1]).then_inc(ex_done, 1)

            e.wait_ge(small_prep, 3)
            e.wait_ge(in_cb, 16)
            e.wait_ge(bt_done, 10)
            weights(0)
            decay(0)
            states(0)
            for h in range(RH):
                if h + 1 < RH:
                    decay(h + 1)
                if h % 2 == 1 and h + 1 < RH:
                    weights((h + 1) // 2)
                    states((h + 1) // 2)
                e.wait_ge(ro_mm, h + 1)
                for t in range(TT):
                    if 2 * h + t >= 2:
                        e.wait_ge(ro_sq, 2 * h + t - 1)
                    e.activation(junk1[:, t, :], bank((5, 2)[h % 2], t * RDV, (t + 1) * RDV), ACT.Square,
                                 accum_out=rss[:, 0, 2 * h + t:2 * h + t + 1]).then_inc(ro_sq, 1)
                if h >= RH - 3:
                    probabilities(h - (RH - 3))

            def pt_out(u):
                e.wait_ge(pt_mm, u + 1)
                e.activation(pt[u % 2][:, :, :].rearrange("p b c -> p (b c)"), bank((1, 4)[u % 2]), ACT.Copy).then_inc(pt_a, 1)

            for u in range(32 + 2):
                if u < 32:
                    if u >= 3:
                        probabilities(u)
                    if u % 8 == 7:
                        g = u // 8
                        e.wait_ge(sk_m, g + 1)
                        e.activation(sinke[:, 8 * g:8 * g + 8], sinkm[:, 8 * g:8 * g + 8], ACT.Exp).then_inc(sk_e, 1)
                if u >= 2 and (u - 2) % 2:
                    if u - 2 >= 2:
                        e.wait_ge(pv_mm, u - 3)
                    pt_out(u - 2)
            e.wait_ge(rr_m, 1)
            e.activation(rss[:, 2, :], rss[:, 1, :], ACT.Sqrt).then_inc(rr_s, 1)

            for g in range(8):
                e.wait_ge(yt_mm, g + 1)
                e.activation(h_hi[:, 2 * g:2 * g + 2, :].rearrange("p k c -> p (k c)"), bank((2, 3, 6, 7)[g % 4]), ACT.Copy).then_inc(yt_hi, 1)

            with e.Fori(0, 2) as i:
                for j in range(2):
                    his(N_OUT + CT * j, i, 2 * CT, CT)
                    e.wait_ge(d_out, i * 2 + (j + 1))
                    for t in range(TT):
                        e.activation(junk2[:, t, :], xr[:, t, ds(i * (2 * CW) + j * CW, CW)], ACT.Square,
                                     accum_out=ss_d[:, t, ds(i * 2 + j, 1)]).then_inc(d_sq, 1)
                    e.wait_ge(d_sq, i * 4 + (2 * j + 2))
            e.wait_ge(dm_done, 2)
            e.activation(st_d[:, 2, :], st_d[:, 1, :], ACT.Sqrt).then_inc(dsd_done, 1)
            for g in range(8):
                for j in range(2):
                    k = 2 * g + j
                    e.wait_ge(em_done, k + 1)
                    e.activation(h_hi[:, k, :], tmp_e[:, k % 4, :], ACT.Copy).then_inc(eh_done, 1)

            def ffn_up(i, first=False):
                his(N_GU, i, 2 * CT, CT)
                e.wait_ge(used, i * 16 + (N_GU + CT))
                if not first:
                    e.wait_ge(act_done, i)
                e.activation(sg[:, :, :].rearrange("p t c -> p (t c)"), ps[:, 0:1024], ACT.Silu).then_inc(sg_done, 1)
                if not first:
                    act_out(i - 1)
                his(N_GU + CT, i, 2 * CT, CT)

            def act_out(i):
                e.wait_ge(at_mm, i + 1)
                for t in range(TT):
                    ins = e.activation(act_t[:, ds(i * 4, 4), t * P:(t + 1) * P], bank(2 + t).rearrange("p (k c) -> p k c", k=4), ACT.Copy)
                ins.then_inc(at_out, 1)

            ffn_up(0, first=True)
            with e.Fori(1, FG) as i:
                ffn_up(i)
            act_out(FG - 1)

            def stage(g, slot):
                e.wait_ge(used, g * CT + (N_DN - CT))
                e.activation(st_hi[slot][:, :, :].rearrange("p k c -> p (k c)"),
                             act_t[:, ds(g * 4, 4), :].rearrange("p k c -> p (k c)"), ACT.Copy).then_inc(sth_done, 1)

            for n in (0, 1):
                e.wait_ge(gf_mm, n + 1)
                e.activation(acc[:, GATE_F + n * CW:GATE_F + (n + 1) * CW], bank((6, 7, 0, 1)[n]), ACT.Copy).then_inc(gf_a, 1)
            e.wait_ge(at_out, FG + 1)
            stage(0, 0)
            stage(1, 1)
            e.dma_start(nf[:, :], norm_final.partition_broadcast(P)).then_inc(in_nf, 16)
            his(N_DN, 0, 0, CT)
            stage(2, 0)
            with e.Fori(0, 4) as i:
                for j in range(2):
                    his(N_DN + CT * (1 + j), i, 2 * CT, CT)
                    stage(i * 2 + (3 + j), (1 + j) % 2)
            his(N_DN + CT * 9, 0, 0, CT)
            his(N_DN + CT * 10, 0, 0, CT - LEAD)
            for n in range(4):
                for t in range(TT):
                    e.wait_ge(f_out, n + 1)
                    if 2 * n + t:
                        e.wait_ge(f_sq, 2 * n + t)
                    e.activation(junk3[:, :], xr[:, t, n * CW:(n + 1) * CW], ACT.Square, accum_out=ss_f[:, t, n:n + 1]).then_inc(f_sq, 1)
            e.wait_ge(fm_done, 2)
            e.activation(st_f[:, 2, :], st_f[:, 1, :], ACT.Sqrt).then_inc(fsd_done, 1)

        @block.vector
        def _(e):
            def lo(t, n):
                e.wait_ge(hi_done, n + 1)
                e.tensor_tensor(w_lo[t % SPLIT][:, :], raw[t % RAW][:, :], w_hi[t % SPLIT][:, :].bitcast(f32),
                                ALU.subtract).then_inc(lo_done, 1)

            def mod_sum(i, per, first, k, col):
                e.wait_ge(mraw_in[first % 2], i * (8 * per) + (first // 2 + 1) * 16)
                for kl in range(2):
                    e.wait_ge(acc_step, i * (2 * per) + (A0 + 2 * first + kl))
                    a = acc[:, ds(col, CW)]
                    e.scalar_tensor_tensor(a, mraw[first % 2][:, kl * CW:(kl + 1) * CW], s32[:, ds(k + kl, 1)], a,
                                           ALU.mult, ALU.add).then_inc(acc_step, 1)

            e.wait_ge(vec_tr, 2)
            e.tensor_copy(vec_t[:, :], bank(2, 0, P)).then_inc(vec_cp, 1)
            e.wait_ge(c4_hi, 1)
            e.tensor_tensor(c4[:, :, :, 1], s32[:, :].rearrange("p (v k) -> p k v", v=2), c4[:, :, :, 0].bitcast(f32),
                            ALU.subtract).then_inc(c4_lo, 1)
            e.wait_ge(sq_done, 4)
            e.tensor_scalar(stat[:, 1, :], stat[:, 0, :], 1.0 / D, EPS, ALU.mult, ALU.add).then_inc(ms_done, 1)
            e.wait_ge(sd_done, 1)
            e.reciprocal(stat[:, 3, :], stat[:, 2, :]).then_inc(rs_done, 1)
            e.wait_ge(rs_done, 1)
            for t in range(4):
                e.tensor_scalar(xin[:, t, :], xin[:, t, :], stat[:, 3, t:t + 1], None, ALU.mult).then_inc(xn_done, 1)
            for g in range(1, 16, 2):
                e.wait_ge(xt_done, g + 1)
                dst = (xt_x if g < 8 else xt_c)[:, g % 4 * 4:g % 4 * 4 + 4, g // 4 % 2 * P:(g // 4 % 2 + 1) * P]
                e.tensor_copy(dst, bank(4 + g % 4).rearrange("p (k c) -> p k c", k=4)).then_inc(xt_d, 1)
            for n in range(LEAD):
                lo(n, n)
            with e.Fori(0, 4) as q:
                for t in range(LEAD, LEAD + KT):
                    lo(t, q * KT + t)
            e.wait_ge(cols_done, 1)
            e.tensor_tensor(modc[:, :, :], bank(0, 0, 4 * KT).rearrange("p (b v) -> p b v", v=2), spread(vec_t[:, 0:2 * KT], 2, 2),
                            ALU.add).then_inc(modc_done, 1)
            e.wait_ge(modc_done, 1)
            e.scalar_tensor_tensor(gm[:, :, :], modc[:, KT:2 * KT, :], 1.0, spread(vec_t[:, 96:112], 2, 2), ALU.add, ALU.mult).then_inc(gm_done, 1)
            e.wait_ge(gm_done, 1)
            with e.Fori(0, 4) as kq:
                for j in range(4):
                    for v, src in enumerate((xt_x, xt_c)):
                        e.tensor_scalar(tmp_s[:, j, v, :], src[:, ds(kq * 4 + j, 1), :].rearrange("p k c -> p (k c)"),
                                        gm[:, ds(kq * 4 + j, 1), v], modc[:, ds(kq * 4 + j, 1), v],
                                        ALU.mult, ALU.add).then_inc(hm_done, 1)
                for j in range(4):
                    e.wait_ge(hh_done, kq * 8 + (2 * j + 2))
                    for v, (h, l) in enumerate(((h_hi, h_lo), (c_hi, c_lo))):
                        e.tensor_tensor(l[:, ds(kq * 4 + j, 1), :].rearrange("p k c -> p (k c)"), tmp_s[:, j, v, :],
                                        h[:, ds(kq * 4 + j, 1), :].rearrange("p k c -> p (k c)").bitcast(f32),
                                        ALU.subtract).then_inc(hl_done, 1)
                e.wait_ge(hl_done, kq * 8 + 8)

            e.wait_ge(acc_bias, 16)
            with e.Fori(0, 2) as i:
                for j in range(2):
                    for t in range(CT):
                        lo(LEAD + t, i * 16 + (N_IN + CT * j + LEAD + t))
                        for u in (2 * t, 2 * t + 1):
                            mod_sum(i, 32, 16 * j + u, 2 * (u % 8), i * (4 * CW) + (2 * j + u // 8) * CW)
            for s in range(5):
                for t in range(CT):
                    lo(LEAD + t, N_IN + CT * (4 + s) + LEAD + t)
                    if s in (1, 3):
                        cc = 8 + s // 2
                        mod_sum(0, 0, 8 * cc + t, 2 * t, cc * CW)

            mix_evac(e, lambda dst, src: e.tensor_copy(dst, src), 1, bt_d)

            def exponents(h):
                e.wait_ge(dexp_done, h + 1)
                if h >= 2:
                    e.wait_ge(dec_done, h - 1)
                e.scalar_tensor_tensor(darg[h % 2][:, :], Bc("ahead"), lg_n[:, 0, h:h + 1], dexp[h % 2][:, :],
                                       ALU.mult, ALU.add).then_inc(darg_done, 1)

            e.wait_ge(in_cb, 16)
            exponents(0)
            exponents(1)
            for n in (2, 3):
                e.wait_ge(gb_done, n + 1)
                e.tensor_copy(acc[:, GATE_M + n * CW:GATE_M + (n + 1) * CW], bank((0, 1, 4, 5)[n])).then_inc(gb_d, 1)
            e.wait_ge(shc_done, 1)
            e.tensor_copy(sh_f[:, :], bank(2, 0, KT)).then_inc(shf_done, 1)

            def query_weights(p):
                e.wait_ge(wtab_done, p + 1)
                if p >= 2:
                    e.wait_ge(ro_mm, 2 * (p - 1))
                e.tensor_tensor(qw[p % 2][:, :, :], spread(qk_t[:, p, 0, :], 1, 2), wtab[p % 2][:, :, :], ALU.mult).then_inc(qw_done, 1)

            def decayed(h):
                e.wait_ge(rsc_mm, h + 1)
                e.wait_ge(dec_done, h + 1)
                if h >= 2:
                    e.wait_ge(ro_mm, h - 1)
                e.tensor_tensor(rp[h % 2][:, :, :].rearrange("p a c -> p (a c)"), bank((1, 4)[h % 2]), dec[h % 2][:, :], ALU.mult).then_inc(rp_done, 1)

            def row_max(u):
                h = 4 * (u // 8) + u % 4
                e.wait_ge(sc_mm, u + 1)
                e.tensor_reduce(rmax[:, u:u + 1], bank((3, 6, 7)[u % 3]), AX.X, ALU.max).then_inc(mx_done, 1)
                e.wait_ge(mx_done, u + 1)
                e.tensor_scalar(nmax[:, u:u + 1], rmax[:, u:u + 1], -SCALE, nsink[:, h:h + 1], ALU.mult, ALU.min).then_inc(nm_done, 1)

            query_weights(0)
            decayed(0)
            for h in range(RH):
                if h + 1 < RH:
                    decayed(h + 1)
                if h + 2 < RH:
                    exponents(h + 2)
                if h % 2 == 1 and h + 1 < RH:
                    query_weights((h + 1) // 2)
                if h >= RH - 3:
                    row_max(h - (RH - 3))
                e.wait_ge(ro_sq, 2 * (h + 1))
                og = proj_y[:, 3 + h // 4, :, h % 4 * RDV:(h % 4 + 1) * RDV]
                e.tensor_tensor(og, bank((5, 2)[h % 2], 0, TT * RDV).rearrange("p (t c) -> p t c", t=TT), og, ALU.mult).then_inc(ro_out, 1)
            e.tensor_scalar(rss[:, 1, :], rss[:, 0, :], 1.0 / RDV, EPS, ALU.mult, ALU.add).then_inc(rr_m, 1)

            for u in range(32 + 3):
                if u < 32:
                    if u >= 3:
                        row_max(u)
                    if u % 8 == 7:
                        g = u // 8
                        e.wait_ge(nm_done, u + 1)
                        e.tensor_tensor(sinkm[:, 8 * g:8 * g + 8].rearrange("p (t h) -> p t h", t=TT),
                                        nmax[:, 8 * g:8 * g + 8].rearrange("p (t h) -> p t h", t=TT),
                                        spread(sink[:, 4 * g:4 * g + 4], 1, TT), ALU.add).then_inc(sk_m, 1)
                if 2 <= u < 34 and u % 2 == 0:
                    v = u - 2
                    e.wait_ge(pt_mm, v + 1)
                    if v >= 2:
                        e.wait_ge(pv_mm, v - 1)
                    e.tensor_copy(pt[v % 2][:, :, :].rearrange("p b c -> p (b c)"), bank((1, 4)[v % 2])).then_inc(pt_d, 1)
                if u >= 10 and (u - 3) % 8 == 7:
                    g = (u - 3) // 8
                    r = slice(8 * g, 8 * g + 8)
                    e.wait_ge(sk_e, g + 1)
                    e.tensor_tensor(den[:, r], rsum[:, r], sinke[:, r], ALU.add).then_inc(dn_done, 1)
                    e.wait_ge(dn_done, g + 1)
                    e.reciprocal(rden[:, r], den[:, r]).then_inc(rd_done, 1)
                    e.wait_ge(rd_done, g + 1)
                    e.wait_ge(pv_mm, 8 * g + 8)
                    e.tensor_tensor(proj_y[:, 1 + g // 2, :, g % 2 * 256:(g % 2 + 1) * 256].rearrange("p t (h c) -> p t h c", h=4),
                                    bank((0, 2)[g % 2]).rearrange("p (t h c) -> p t h c", t=TT, h=4),
                                    spread(rden[:, r].rearrange("p (t h) -> p t h", t=TT), 3, DH), ALU.mult).then_inc(ya_done, 1)
            e.wait_ge(rr_s, 1)
            e.reciprocal(rss[:, 3, :], rss[:, 2, :]).then_inc(rr_r, 1)
            e.wait_ge(rr_r, 1)
            rs = rss[:, 3, :].rearrange("p (h t) -> p t h", t=TT)
            for hq in range(2):
                for t in range(TT):
                    og = proj_y[:, 3 + hq, t, :].rearrange("p (h c) -> p h c", h=4)
                    e.tensor_tensor(og, og, spread(rs[:, t, 4 * hq:4 * hq + 4], 2, RDV), ALU.mult).then_inc(yr_done, 1)
            for g in range(8):
                e.wait_ge(yt_hi, g + 1)
                e.tensor_tensor(h_lo[:, 2 * g:2 * g + 2, :].rearrange("p k c -> p (k c)"), bank((2, 3, 6, 7)[g % 4]),
                                h_hi[:, 2 * g:2 * g + 2, :].rearrange("p k c -> p (k c)").bitcast(f32), ALU.subtract).then_inc(yt_lo, 1)

            e.wait_ge(in_xr, 16)
            e.sem_inc(d_scaled, 1)
            with e.Fori(0, 2) as i:
                for j in range(2):
                    for t in range(CT):
                        lo(LEAD + t, i * 16 + (N_OUT + CT * j + LEAD + t))
                        if j == 0:
                            mod_sum(i, 8, 80 + t, 2 * t, i * CW + 10 * CW)
                    e.wait_ge(used, i * 16 + (N_OUT + CT * (j + 1)))
                    e.tensor_tensor(tmp_d[:, :, :], ps[:, j * 2048:j * 2048 + 1024].rearrange("p (t c) -> p t c", t=TT),
                                    spread(acc[:, ds(i * (2 * CW) + (GATE_M + j * CW), CW)], 1, TT), ALU.mult).then_inc(d_scaled, 1)
                    e.wait_ge(d_scaled, i * 2 + (j + 2))
                    xc = xr[:, :, ds(i * (2 * CW) + j * CW, CW)]
                    e.tensor_tensor(xc, tmp_d[:, :, :], xc, ALU.add).then_inc(d_out, 1)
                    e.wait_ge(d_out, i * 2 + (j + 1))
            e.wait_ge(scc_done, 1)
            e.scalar_tensor_tensor(gm_f[:, :], bank(0, 0, KT), 1.0, vec_t[:, 112:128], ALU.add, ALU.mult).then_inc(gmf_done, 1)
            e.wait_ge(d_sq, 8)
            e.tensor_reduce(st_d[:, 0, :], ss_d[:, :, :], AX.X, ALU.add).then_inc(dm_done, 1)
            e.wait_ge(dm_done, 1)
            e.tensor_scalar(st_d[:, 1, :], st_d[:, 0, :], 1.0 / D, EPS, ALU.mult, ALU.add).then_inc(dm_done, 1)
            e.wait_ge(dsd_done, 1)
            e.reciprocal(st_d[:, 3, :], st_d[:, 2, :]).then_inc(drs_done, 1)
            e.wait_ge(drs_done, 1)
            for t in range(TT):
                e.tensor_scalar(xn[:, t, :], xr[:, t, :], st_d[:, 3, t:t + 1], None, ALU.mult).then_inc(xn2_done, 1)
            e.wait_ge(gmf_done, 1)

            def modulated(k):
                e.wait_ge(et_mm, k // 2 + 1)
                if k >= 4:
                    e.wait_ge(el_done, k - 3)
                e.tensor_scalar(tmp_e[:, k % 4, :], bank((2, 3, 6, 7)[k // 2 % 4], k % 2 * 256, k % 2 * 256 + 256),
                                gm_f[:, k:k + 1], sh_f[:, k:k + 1], ALU.mult, ALU.add).then_inc(em_done, 1)

            modulated(0)
            modulated(1)
            for k in range(KT):
                if k % 2 == 0 and k + 2 < KT:
                    modulated(k + 2)
                    modulated(k + 3)
                e.wait_ge(eh_done, k + 1)
                e.tensor_tensor(h_lo[:, k, :], tmp_e[:, k % 4, :], h_hi[:, k, :].bitcast(f32), ALU.subtract).then_inc(el_done, 1)

            def ffn_up(i, mods, first=False):
                for j in range(2):
                    for t in range(CT):
                        lo(LEAD + t, i * 16 + (N_GU + CT * j + LEAD + t))
                        if mods and j == 0 and t % 2 == 0:
                            u = t // 2
                            mod_sum(i, 4, 92 + u, i * 2 - 2, GATE_F + u * CW)
                e.wait_ge(used, i * 16 + (N_GU + 2 * CT))
                e.wait_ge(sg_done, i + 1)
                if not first:
                    e.wait_ge(at_mm, i)
                e.tensor_tensor(act[:, :, :].rearrange("p t c -> p (t c)"), ps[:, 4 * CW:6 * CW],
                                sg[:, :, :].rearrange("p t c -> p (t c)"), ALU.mult).then_inc(act_done, 1)

            ffn_up(0, False, first=True)
            e.wait_ge(acc_bias2, 16)
            with e.Fori(1, 9) as i:
                ffn_up(i, True)
            with e.Fori(9, FG) as i:
                ffn_up(i, False)

            def stage(g, slot):
                e.wait_ge(sth_done, g + 1)
                e.tensor_tensor(st_lo[slot][:, :, :].rearrange("p k c -> p (k c)"), act_t[:, ds(g * 4, 4), :].rearrange("p k c -> p (k c)"),
                                st_hi[slot][:, :, :].rearrange("p k c -> p (k c)").bitcast(f32), ALU.subtract).then_inc(stl_done, 1)

            for n in (2, 3):
                e.wait_ge(gf_mm, n + 1)
                e.tensor_copy(acc[:, GATE_F + n * CW:GATE_F + (n + 1) * CW], bank((6, 7, 0, 1)[n])).then_inc(gf_d, 1)
            stage(0, 0)
            stage(1, 1)
            for t in range(CT):
                lo(LEAD + t, N_DN + LEAD + t)
            stage(2, 0)
            with e.Fori(0, 4) as i:
                for j in range(2):
                    for t in range(CT):
                        lo(LEAD + t, i * 16 + (N_DN + CT * (1 + j) + LEAD + t))
                    stage(i * 2 + (3 + j), (1 + j) % 2)
            for t in range(2 * CT - LEAD):
                lo(LEAD + t, N_DN + 9 * CT + LEAD + t)
            for n in range(4):
                e.wait_ge(used, N_DN + 10 * CT + 2 * n + 2)
                if n:
                    e.wait_ge(f_out, n)
                e.tensor_tensor(tmp_f[:, :, :], ps[:, n * 1024:(n + 1) * 1024].rearrange("p (t c) -> p t c", t=TT),
                                spread(acc[:, GATE_F + n * CW:GATE_F + (n + 1) * CW], 1, TT), ALU.mult).then_inc(f_scaled, 1)
                e.wait_ge(f_scaled, n + 1)
                xc = xr[:, :, n * CW:(n + 1) * CW]
                e.tensor_tensor(xc, tmp_f[:, :, :], xc, ALU.add).then_inc(f_out, 1)
            e.wait_ge(f_sq, 8)
            e.tensor_reduce(st_f[:, 0, :], ss_f[:, :, :], AX.X, ALU.add).then_inc(fm_done, 1)
            e.wait_ge(fm_done, 1)
            e.tensor_scalar(st_f[:, 1, :], st_f[:, 0, :], 1.0 / D, EPS, ALU.mult, ALU.add).then_inc(fm_done, 1)
            e.wait_ge(fsd_done, 1)
            e.reciprocal(st_f[:, 3, :], st_f[:, 2, :]).then_inc(frs_done, 1)
            e.wait_ge(frs_done, 1)
            e.wait_ge(in_nf, 16)
            for t in range(TT):
                e.scalar_tensor_tensor(xr[:, t, :], xr[:, t, :], st_f[:, 3, t:t + 1], nf[:, :], ALU.mult, ALU.mult).then_inc(fin_done, 1)

        @block.tensor
        def _(pe):
            def split_product(dst, a_hi, a_lo, w, w2, start, stop):
                pe.matmul(dst, a_hi, w, start=start, stop=False)
                pe.matmul(dst, a_hi, w2, start=False, stop=False)
                return pe.matmul(dst, a_lo, w, start=False, stop=stop)

            def chunk(i, per, first, operands, ready=None, each=1):
                for t in range(CT):
                    pe.wait_ge(lo_done, i * per + (first + t + 1))
                    for kl in range(2):
                        k = 2 * t + kl
                        if ready is not None:
                            pe.wait_ge(ready, (k + 1) * each if each else t + 1)
                        cols = slice(kl * CW, (kl + 1) * CW)
                        for hi, lo, tok, b in operands:
                            ins = split_product(bank(b), hi[:, k, tok:tok + P], lo[:, k, tok:tok + P],
                                                w_hi[t % SPLIT][:, cols], w_lo[t % SPLIT][:, cols], k == 0, k == KT - 1)
                    ins.then_inc(used, 1)

            def latents(b):
                return [(h_hi, h_lo, 0, b), (h_hi, h_lo, P, b + 1)]

            pe.wait_ge(in_rows, 80)
            pe.wait_ge(in_ca, 16)
            pe.transpose(bank(3, 0, 2 * KT), rows_b[:, :], ident[0:2 * KT, 0:2 * KT]).then_inc(vec_tr, 1)
            pe.transpose(bank(2, 0, P), rows_a[:, :], ident).then_inc(vec_tr, 1)
            for g in range(16):
                pe.wait_ge(xn_done, g // 4 + 1)
                if g >= 4:
                    pe.wait_ge(xt_d if g % 2 else xt_a, (g - 4) // 2 + 1)
                for b in range(4):
                    k = g % 4 * 4 + b
                    ins = pe.transpose(bank(4 + g % 4, b * P, (b + 1) * P), xin[:, g // 4, k * P:(k + 1) * P], ident)
                ins.then_inc(xt_done, 1)
            pe.wait_ge(xt_a, 8)
            pe.wait_ge(xt_d, 8)
            pe.wait_ge(vec_cp, 1)
            pe.wait_ge(c4_lo, 1)
            with pe.Fori(0, 2) as i:
                for j in range(2):
                    if j:
                        pe.wait_ge(rows_done, i * 2 + 1)
                    for t in range(KT):
                        pe.wait_ge(lo_done, i * (2 * KT) + (j * KT + t + 1))
                        lhs = c4[:, t, :, :].rearrange("p v s -> p (v s)")
                        for b in range(2):
                            dst = bank(2 * j + b)[0:4, :]
                            cols = slice(b * CW, (b + 1) * CW)
                            pe.matmul(dst, lhs, w_hi[t % SPLIT][:, cols], start=t == 0, stop=False)
                            ins = pe.matmul(dst, lhs, w_lo[t % SPLIT][:, cols], start=False, stop=t == KT - 1)
                        ins.then_inc(used, 1)
                pe.wait_ge(rows_done, i * 2 + 2)
            pe.wait_ge(rows_done, 5)
            for b in range(2 * KT):
                ins = pe.matmul(bank(0, 2 * b, 2 * b + 2), mod_rows[0:4, b * P:(b + 1) * P], A("sel")[0:4, :], start=True, stop=True)
            ins.then_inc(cols_done, 1)

            with pe.Fori(0, 2) as i:
                for j in range(2):
                    if j:
                        pe.wait_ge(proj_out, i * 2 + 1)
                    chunk(i, 16, N_IN + CT * j, latents(4 * j) + [(c_hi, c_lo, 0, 4 * j + 2), (c_hi, c_lo, P, 4 * j + 3)], hl_done, 2)
                pe.wait_ge(proj_out, i * 2 + 2)
            chunk(0, 0, N_IN + 4 * CT, latents(0))
            with pe.Fori(0, 2) as i:
                pe.wait_ge(proj_out, i * 2 + 5)
                chunk(i, 16, N_IN + 5 * CT, latents(4))
                pe.wait_ge(proj_out, i * 2 + 6)
                chunk(i, 16, N_IN + 6 * CT, latents(0))

            for g in range(10):
                pe.wait_ge(rope_done, 12 if g < 4 else 20)
                if g >= 4:
                    pe.wait_ge(bt_d if g % 2 else bt_a, (g - 4) // 2 + 1)
                b = BT_BANKS[g % 4]
                for t in range(TT):
                    lohi = [(t * P, (t + 1) * P), ((2 + t) * P, (3 + t) * P)]
                    if g < 4:
                        srcs = [proj_y[:, 0, t, g * P:(g + 1) * P], proj_x[:, 0, t, g * P:(g + 1) * P]]
                    elif g < 8:
                        srcs = [proj_y[:, 1 + pr // 4, t, pr % 4 * P:(pr % 4 + 1) * P] for pr in (2 * g - 8, 2 * g - 7)]
                    else:
                        srcs = [pj[:, 3, t, (g - 8) * P:(g - 7) * P] for pj in (proj_x, proj_c)]
                    for (lo_, hi_), src in zip(lohi, srcs):
                        ins = pe.transpose(bank(b, lo_, hi_), src, ident)
                ins.then_inc(bt_done, 1)
            pe.wait_ge(acc_step, A0 + 2 * 32)
            pe.wait_ge(proj_out, 10)
            for n in range(4):
                pe.matmul(bank((0, 1, 4, 5)[n]), A("ones"), acc[:, GATE_M + n * CW:GATE_M + (n + 1) * CW], start=True, stop=True).then_inc(gb_done, 1)
            pe.wait_ge(acc_step, A0 + 2 * 64)
            pe.wait_ge(bt_a, 5)
            pe.wait_ge(bt_d, 5)
            for b in range(KT):
                ins = pe.matmul(bank(2, b, b + 1), acc[:, SHIFT_F + b * P:SHIFT_F + (b + 1) * P], A("ones", 0, 1), start=True, stop=True)
            ins.then_inc(shc_done, 1)

            def states(p):
                if p:
                    pe.wait_ge(st_cp, p)
                for s in range(2):
                    h = 2 * p + s
                    for d in range(2):
                        for lt in range(TT):
                            ins = pe.matmul(ps[64 * s:64 * s + 64, d * RDV:(d + 1) * RDV], ckw[:, lt, d, h, :],
                                            proj_c[:, 1 + h // 4, lt, h % 4 * RDV:(h % 4 + 1) * RDV], start=lt == 0, stop=lt == TT - 1)
                ins.then_inc(st_mm, 1)

            def scores(h):
                if h >= 2:
                    pe.wait_ge(rp_done, h - 1)
                q = slice(64 * (h % 2), 64 * (h % 2) + 64)
                for jt in range(TT):
                    ins = pe.matmul(bank((1, 4)[h % 2], jt * SEQ, (jt + 1) * SEQ), qk_t[q, h // 2, 1, jt * P:(jt + 1) * P],
                                    qk_t[q, h // 2, 0, :], start=True, stop=True)
                ins.then_inc(rsc_mm, 1)

            def attention_scores(u):
                t, kv = u % 8 // 4, u // 8
                q = slice(64 * (kv % 2), 64 * (kv % 2) + 64)
                if u >= 3:
                    pe.wait_ge(ex_done, u - 2)
                b = (3, 6, 7)[u % 3]
                pe.matmul(bank(b), aq_t[q, kv // 2 * 4 + u % 4, t * P:(t + 1) * P], ak_t[q, kv // 2, :], start=True, stop=False)
                far = slice(P, 2 * P) if t == 0 else slice(0, P)
                pe.matmul(bank(b, far.start, far.stop), ident, A("mask", t * P, (t + 1) * P), start=False, stop=True).then_inc(sc_mm, 1)

            pe.wait_ge(gb_a, 2)
            pe.wait_ge(gb_d, 2)
            pe.wait_ge(ckw_done, 4)
            states(0)
            scores(0)
            for h in range(RH):
                if h + 1 < RH:
                    scores(h + 1)
                if h % 2 == 1 and h + 1 < RH:
                    states((h + 1) // 2)
                if h >= RH - 3:
                    attention_scores(h - (RH - 3))
                pe.wait_ge(rp_done, h + 1)
                pe.wait_ge(qw_done, h // 2 + 1)
                pe.wait_ge(st_cp, h // 2 + 1)
                if h == 1:
                    pe.wait_ge(shf_done, 1)
                if h >= 2:
                    pe.wait_ge(ro_out, h - 1)
                q = slice(64 * (h % 2), 64 * (h % 2) + 64)
                for t in range(TT):
                    dst = bank((5, 2)[h % 2], t * RDV, (t + 1) * RDV)
                    tok = slice(t * P, (t + 1) * P)
                    for jt in range(TT):
                        pe.matmul(dst, rp[h % 2][:, jt, tok], proj_x[:, 1 + h // 4, jt, h % 4 * RDV:(h % 4 + 1) * RDV], start=jt == 0, stop=False)
                    for d in range(2):
                        ins = pe.matmul(dst, qw[h // 2 % 2][q, d, tok], s_sb[h // 2 % 2][q, d, :], start=False, stop=d == 1)
                ins.then_inc(ro_mm, 1)

            for u in range(32 + 3):
                if 3 <= u < 32:
                    attention_scores(u)
                if 2 <= u < 34:
                    v = u - 2
                    pe.wait_ge(ex_done, v + 1)
                    if v >= 2:
                        pe.wait_ge(pt_a if v % 2 else pt_d, v // 2)
                    for kb in range(4):
                        ins = pe.transpose(bank((1, 4)[v % 2], kb * P, (kb + 1) * P), prob[v % 3][:, kb * P:(kb + 1) * P], ident)
                    ins.then_inc(pt_mm, 1)
                if u >= 3:
                    v = u - 3
                    g = v // 8
                    pe.wait_ge(pt_a if v % 2 else pt_d, v // 2 + 1)
                    if v % 8 == 0:
                        if g >= 2:
                            pe.wait_ge(ya_done, g - 1)
                        else:
                            pe.wait_ge(ro_out, RH)
                    for kb in range(4):
                        pj = proj_x if kb < 2 else proj_c
                        ins = pe.matmul(bank((0, 2)[g % 2], v % 8 * DH, (v % 8 + 1) * DH), pt[v % 2][:, kb, :],
                                        pj[:, 3, kb % 2, 256 + g * DH:256 + (g + 1) * DH], start=kb == 0, stop=kb == 3)
                    ins.then_inc(pv_mm, 1)

            pe.wait_ge(ya_done, 4)
            pe.wait_ge(ex_done, 32)
            for g in range(8):
                if g >= 4:
                    pe.wait_ge(yr_done, 4)
                    pe.wait_ge(yt_lo, g - 3)
                for kl in range(2):
                    k = (8 + 2 * g + kl) % 16
                    s, col = (1 + (k - 8) // 4, k % 4 * P) if k >= 8 else (3 + k // 4, k % 4 * P)
                    for t in range(TT):
                        ins = pe.transpose(bank((2, 3, 6, 7)[g % 4], kl * 256 + t * P, kl * 256 + (t + 1) * P), proj_y[:, s, t, col:col + P], ident)
                ins.then_inc(yt_mm, 1)
            with pe.Fori(0, 2) as i:
                for j in range(2):
                    if j:
                        pe.wait_ge(d_scaled, i * 2 + 1)
                    chunk(i, 16, N_OUT + CT * j, latents(4 * j), yt_lo, 0)
                pe.wait_ge(d_scaled, i * 2 + 2)
            pe.wait_ge(acc_step, A0 + 2 * 96)
            for b in range(KT):
                ins = pe.matmul(bank(0, b, b + 1), acc[:, SCALE_F + b * P:SCALE_F + (b + 1) * P], A("ones", 0, 1), start=True, stop=True)
            ins.then_inc(scc_done, 1)
            pe.wait_ge(xn2_done, 2)
            for g in range(8):
                if g >= 4:
                    pe.wait_ge(em_done, 2 * (g - 3))
                for kl in range(2):
                    k = 2 * g + kl
                    for t in range(TT):
                        ins = pe.transpose(bank((2, 3, 6, 7)[g % 4], kl * 256 + t * P, kl * 256 + (t + 1) * P), xn[:, t, k * P:(k + 1) * P], ident)
                ins.then_inc(et_mm, 1)

            def turn(i):
                pe.wait_ge(act_done, i + 1)
                pe.wait_ge(at_out, i + 1)
                for t in range(TT):
                    for b in range(4):
                        ins = pe.transpose(bank(2 + t, b * P, (b + 1) * P), act[:, t, b * P:(b + 1) * P], ident)
                ins.then_inc(at_mm, 1)

            pe.wait_ge(gmf_done, 1)
            pe.wait_ge(d_scaled, 5)
            chunk(0, 0, N_GU, latents(0), el_done, 1)
            chunk(0, 0, N_GU + CT, latents(4))
            with pe.Fori(1, FG) as i:
                pe.wait_ge(sg_done, i)
                chunk(i, 16, N_GU, latents(0))
                turn(i - 1)
                chunk(i, 16, N_GU + CT, latents(4))
            turn(FG - 1)
            pe.wait_ge(acc_step, A0 + 2 * 128)
            pe.wait_ge(sg_done, FG)
            for n in range(4):
                pe.matmul(bank((6, 7, 0, 1)[n]), A("ones"), acc[:, GATE_F + n * CW:GATE_F + (n + 1) * CW], start=True, stop=True).then_inc(gf_mm, 1)

            def group(g, i, per, first, slot, start=False, stop=False):
                pe.wait_ge(stl_done, g + 1)
                for t in range(CT):
                    pe.wait_ge(lo_done, i * per + (first + t + 1))
                    for kl in range(2):
                        k = t % 2 * 2 + kl
                        cols = slice(kl * CW, (kl + 1) * CW)
                        for tt in range(TT):
                            ins = split_product(bank(t // 2 * 2 + tt), st_hi[slot][:, k, tt * P:(tt + 1) * P],
                                                st_lo[slot][:, k, tt * P:(tt + 1) * P], w_hi[t % SPLIT][:, cols],
                                                w_lo[t % SPLIT][:, cols], start and k == 0, stop and k == 3)
                    ins.then_inc(used, 1)

            pe.wait_ge(gf_a, 2)
            pe.wait_ge(gf_d, 2)
            pe.wait_ge(at_out, FG + 1)
            group(0, 0, 0, N_DN, 0, start=True)
            with pe.Fori(0, 4) as i:
                for j in range(2):
                    group(i * 2 + (1 + j), i, 16, N_DN + CT * (1 + j), (1 + j) % 2)
            group(9, 0, 0, N_DN + 9 * CT, 1)
            group(10, 0, 0, N_DN + 10 * CT, 0, stop=True)


def constants(np):
    a = np.zeros((P, NCA), np.float32)
    b = np.zeros((P, NCB), np.float32)

    def put(dst, cols, name, v):
        s, e = cols[name]
        dst[:, s:e] = np.asarray(v).reshape(P, e - s)

    p = np.arange(P)
    tok = np.arange(SEQ).reshape(TT, P)
    put(a, CA, "ident", np.eye(P))
    put(a, CA, "ones", np.ones((P, P)))
    far = np.where(p[None, :] > p[:, None], -1e30, 0.0), np.where(p[:, None] > p[None, :], -1e30, 0.0)
    put(a, CA, "mask", np.concatenate(far, 1))
    inv = np.float32(10000.0) ** (-np.arange(32, dtype=np.float32) / np.float32(32))
    ang = (tok[..., None].astype(np.float32) * inv).transpose(1, 0, 2)
    for name, scale in (("rq", RDK ** -0.5), ("rk", 1.0)):
        put(a, CA, name + "_cos", scale * np.cos(ang))
        put(a, CA, name + "_sin", scale * np.sin(ang))
    inv = np.float32(10000.0) ** (-np.arange(16, dtype=np.float32) / np.float32(16))
    pos = np.stack([tok // 64, tok % 64], -1).astype(np.float32)
    ang = (pos[..., None] * inv).transpose(1, 0, 2, 3)
    put(a, CA, "ax_cos", np.cos(ang))
    put(a, CA, "ax_sin", np.sin(ang))
    ctx = np.arange(CTX).reshape(TT, P)
    put(a, CA, "expo", np.stack([CTX - 1 - ctx, ctx], -1).transpose(1, 0, 2))
    a[0:4, CA["sel"][0]:CA["sel"][1]] = [[1, 0], [1, 0], [0, 1], [0, 1]]
    rel = np.arange(SEQ)[None, None, :] - tok.T[:, :, None]
    put(b, CB, "ahead", np.maximum(rel, 0))
    put(b, CB, "behind", np.maximum(-rel, 0))
    put(b, CB, "pos_f", np.broadcast_to(np.arange(SEQ) + 1, (P, SEQ)))
    put(b, CB, "pos_b", np.broadcast_to(SEQ - np.arange(SEQ), (P, SEQ)))
    return a, b


_INS = ["x", "c", "ctx", "c_ctx", "w_mod", "b_mod", "norm_mix", "norm_ffn", "w_in", "ret_decay", "attn_sink",
        "w_out", "w_gate", "w_up", "w_down", "norm_final"]


def kernel(**inputs):
    import numpy as np
    import concourse.bacc as bacc
    from concourse.bass_utils import run_bass_kernel_spmd

    nc = bacc.Bacc("TRN2", target_bir_lowering=False, num_devices=1)
    const_a, const_b = constants(np)
    arrays = {name: np.ascontiguousarray(inputs[name]) for name in _INS}
    arrays["const_a"], arrays["const_b"] = const_a, const_b
    args = [nc.dram_tensor(name, a.shape, mybir.dt.from_np(a.dtype), kind="ExternalInput").ap()
            for name, a in arrays.items()]
    out = nc.dram_tensor("out", (1, SEQ, D), mybir.dt.float32, kind="ExternalOutput").ap()
    build(nc, *args, out)
    r = run_bass_kernel_spmd(nc, [arrays], core_ids=[0])
    return r.results[0]["out"]
```

```python
import concourse.bass as bass
from concourse import mybir
from contextlib import ExitStack

P = 128
SEQ, CTX, D = 256, 256, 2048
KT = D // P
TT = SEQ // P
RH, RDK, RDV = 8, 64, 128
AH, KVH, DH = 16, 4, 64
DFF = 5632
FG = DFF // 512
CW = 512
RAW, SPLIT, LEAD = 8, 4, 4
CT = KT // 2
EPS = 1e-6
SCALE = DH ** -0.5

N_MOD = 0
N_IN = N_MOD + 4 * KT
N_OUT = N_IN + 9 * CT
N_GU = N_OUT + 4 * CT
N_DN = N_GU + 2 * FG * CT
N_END = N_DN + FG * CT

CA = {}
CB = {}
_at = 0
for _n, _w in (("ident", P), ("ones", P), ("mask", 2 * P), ("rq_cos", 64), ("rq_sin", 64), ("rk_cos", 64),
               ("rk_sin", 64), ("ax_cos", 64), ("ax_sin", 64), ("expo", 4), ("sel", 2)):
    CA[_n] = (_at, _at + _w)
    _at += _w
NCA = _at
_at = 0
for _n, _w in (("ahead", 512), ("behind", 512), ("pos_f", 256), ("pos_b", 256)):
    CB[_n] = (_at, _at + _w)
    _at += _w
NCB = _at


def build(nc, x, c, ctx, c_ctx, w_mod, b_mod, norm_mix, norm_ffn, w_in, ret_decay, attn_sink,
          w_out, w_gate, w_up, w_down, norm_final, const_a, const_b, out):
    f32, f32r = mybir.dt.float32, mybir.dt.float32r
    ACT, ALU, AX = mybir.ActivationFunctionType, mybir.AluOpType, mybir.AxisListType
    ds = bass.ds
    stack = ExitStack()
    with stack:
        base = (nc.sbuf_base + 63) // 64 * 64
        at = [base]

        def place(name, shape, dt=f32, offset=None):
            size = 4
            for n in shape[1:]:
                size *= n
            if offset is None:
                offset = at[0]
                at[0] += (size + 31) // 32 * 32
            assert offset + size <= nc.sbuf_usable_end, name
            return nc.alloc_sbuf_tensor_at(name, shape, dt, offset=offset)

        K1 = 1024
        ca = place("const_a_sb", [P, NCA])
        cb_at = at[0]
        cb = place("const_b_sb", [P, NCB])
        h_at = at[0]
        h_hi = place("h_hi", [P, KT, SEQ], f32r)
        h_lo = place("h_lo", [P, KT, SEQ], f32r)
        px_at = at[0]
        proj_x = place("proj_x", [P, 4, TT, CW])
        ch_at = at[0]
        c_hi = place("c_hi", [P, KT, CTX], f32r)
        c_lo = place("c_lo", [P, KT, CTX], f32r)
        pc_at = at[0]
        proj_c = place("proj_c", [P, 4, TT, CW])
        raw = [place(f"raw{s}", [P, 1024]) for s in range(RAW)]
        w_hi = [place(f"w_hi{s}", [P, 1024], f32r) for s in range(SPLIT)]
        w_lo = [place(f"w_lo{s}", [P, 1024], f32r) for s in range(SPLIT)]
        m_at = at[0]
        mraw = [place(f"mraw{s}", [P, 1024])[:, :] for s in range(2)]
        mraw += [proj_x[:, 3, :, :].rearrange("p t c -> p (t c)"), proj_c[:, 3, :, :].rearrange("p t c -> p (t c)")]
        acc_at = at[0]
        acc = place("acc", [P, 3 * D])
        rows_a = place("rows_a", [P, P])
        rows_b = place("rows_b", [2 * KT, P])
        vec_t = place("vec_t", [P, P])
        s32 = place("s32", [P, 2 * KT])
        c4 = place("c4", [P, KT, 2, 2], f32r)
        modc = place("modc", [P, 2 * KT, 2])
        gm = place("gm", [P, 2, KT // 2, 2])
        stat = place("stat", [P, 4, 4])
        lg_raw = place("lg_raw", [P, 2, RH])
        lg_e = place("lg_e", [P, 2, RH])
        lg_n = place("lg_n", [P, 2, RH])
        lg_p = place("lg_p", [P, 2, RH // 2])
        sink = place("sink", [P, AH])
        nsink = place("nsink", [P, AH])
        wexp = place("wexp", [P, TT, 2, RH])
        wck = place("wck", [P, TT, 2, RH])
        rmax = place("rmax", [P, 32])
        nmax = place("nmax", [P, 32])
        rsum = place("rsum", [P, 32])
        sinkm = place("sinkm", [P, 32])
        sinke = place("sinke", [P, 32])
        den = place("den", [P, 32])
        rden = place("rden", [P, 32])
        rss = place("rss", [P, 4, 16])
        sh_f = place("sh_f", [P, KT])
        gm_f = place("gm_f", [P, KT])
        ss_d = place("ss_d", [P, TT, 4])
        st_d = place("st_d", [P, 4, TT])
        ss_f = place("ss_f", [P, TT, 4])
        st_f = place("st_f", [P, 4, TT])

        ident_r = place("ident_r", [P, P], f32r)
        mask_r = place("mask_r", [P, 2 * P], f32r)

        xin = place("xin", [P, 4, D], offset=h_at)
        xt_x = place("xt_x", [P, KT, SEQ], offset=px_at)
        xt_c = place("xt_c", [P, KT, CTX], offset=pc_at)
        mod_rows = place("mod_rows", [4, 1024], offset=acc_at + 16 * K1)
        junk0 = place("junk0", [P, D], offset=m_at)
        tmp_s = place("tmp_s", [P, 4, 2, 256], offset=m_at)
        proj_y = place("proj_y", [P, 5, TT, CW], offset=ch_at)
        rope_t = place("rope_t", [P, 4, 256], offset=ch_at + 20 * K1)
        ckw = place("ckw", [P, TT, 2, RH, RDK], offset=ch_at + 24 * K1)
        aq_t = place("aq_t", [P, 8, SEQ], offset=h_at)
        qk_t = place("qk_t", [P, 4, 2, SEQ], offset=h_at + 8 * K1)
        ak_t = place("ak_t", [P, KVH // 2, SEQ + CTX], offset=h_at + 16 * K1)
        darg = [place(f"darg{s}", [P, 512], offset=h_at + (24 + 2 * s) * K1) for s in range(2)]
        qw = [place(f"qw{s}", [P, 2, SEQ], offset=h_at + (28 + 2 * s) * K1) for s in range(2)]
        dec = [place(f"dec{s}", [P, 512], offset=px_at + 2 * s * K1) for s in range(2)]
        rp = [place(f"rp{s}", [P, 2, SEQ], offset=pc_at + 2 * s * K1) for s in range(2)]
        wtab = [place(f"wtab{s}", [P, 2, SEQ], offset=ch_at + 2 * s * K1) for s in range(2)]
        s_sb = [place(f"s_sb{s}", [P, 2, RDV], offset=ch_at + (20 + s) * K1) for s in range(2)]
        pt = [place(f"pt{s}", [P, 4, P], offset=px_at + 2 * s * K1) for s in range(2)]
        prob = [place("prob0", [P, 512], offset=h_at + 20 * K1), place("prob1", [P, 512], offset=h_at + 22 * K1),
                place("prob2", [P, 512], offset=ch_at + 22 * K1)]
        dexp = [place(f"dexp{s}", [P, 512], offset=m_at + 2 * s * K1) for s in range(2)]
        junk1 = place("junk1", [P, 2, P], offset=m_at + 4 * K1)
        xr = place("xr", [P, TT, D], offset=px_at)
        tmp_d = place("tmp_d", [P, TT, CW], offset=pc_at)
        junk2 = place("junk2", [P, TT, CW], offset=pc_at + 4 * K1)
        xn = place("xn", [P, TT, D], offset=ch_at)
        tmp_e = place("tmp_e", [P, 4, 256], offset=pc_at + 8 * K1)
        act_t = place("act_t", [P, 4 * FG, SEQ], offset=ch_at)
        act = place("act", [P, TT, CW], offset=ch_at + 44 * K1)
        sg = place("sg", [P, TT, CW], offset=cb_at)
        st_hi = [place(f"st_hi{s}", [P, 4, SEQ], f32r, offset=acc_at + 4 * s * K1) for s in range(2)]
        st_lo = [place(f"st_lo{s}", [P, 4, SEQ], f32r, offset=acc_at + (16 + 4 * s) * K1) for s in range(2)]
        nf = place("nf", [P, D], offset=h_at)
        tmp_f = place("tmp_f", [P, TT, CW], offset=h_at + 8 * K1)
        junk3 = place("junk3", [P, CW], offset=h_at + 12 * K1)
        fin = place("fin", [P, TT, D], offset=h_at + 16 * K1)

        ps = stack.enter_context(nc.psum_tensor("ps", [P, 8 * CW], f32))

        def bank(b, lo=0, hi=CW):
            return ps[:, b * CW + lo:b * CW + hi]

        def A(name, lo=0, hi=None):
            s, e = CA[name]
            return ca[:, s + lo:(s + hi if hi is not None else e)]

        def Bc(name):
            s, e = CB[name]
            return cb[:, s:e]

        ident = A("ident")

        def spread(ap, axis, n):
            ap = ap.unsqueeze(axis)
            shape = list(ap.shape)
            shape[axis] = n
            return ap.to_broadcast(shape)

        def sem(name):
            return stack.enter_context(nc.semaphore(name))

        raw_in = [sem(f"raw_in{s}") for s in range(RAW)]
        hi_done = sem("hi_done")
        lo_done = sem("lo_done")
        used = sem("used")
        mraw_in = [sem(f"mraw_in{s}") for s in range(4)]
        acc_step = sem("acc_step")
        in_rows, in_small, in_ca, in_cb = sem("in_rows"), sem("in_small"), sem("in_ca"), sem("in_cb")
        in_x = [sem(f"in_x{t}") for t in range(4)]
        vec_tr, vec_cp, silu_c, c4_hi, c4_lo = sem("vec_tr"), sem("vec_cp"), sem("silu_c"), sem("c4_hi"), sem("c4_lo")
        sq_done, ms_done, sd_done, rs_done, xn_done = sem("sq_done"), sem("ms_done"), sem("sd_done"), sem("rs_done"), sem("xn_done")
        xt_done, xt_a, xt_d = sem("xt_done"), sem("xt_a"), sem("xt_d")
        rows_done, cols_done, modc_done, gm_done = sem("rows_done"), sem("cols_done"), sem("modc_done"), sem("gm_done")
        hm_pool, hh_pool, hl_pool = sem("hm_pool"), sem("hh_pool"), sem("hl_pool")
        hm_done, hh_done, hl_done = sem("hm_done"), sem("hh_done"), sem("hl_done")
        proj_out = sem("proj_out")
        acc_bias, acc_zero_s, acc_bias_s = sem("acc_bias"), sem("acc_zero_s"), sem("acc_bias_s")
        ckw_done, gb_d = sem("ckw_done"), sem("gb_d")
        lg_done, pool_step, rope_done, wck_done = sem("lg_done"), sem("pool_step"), sem("rope_done"), sem("wck_done")
        wexp_done, small_prep = sem("wexp_done"), sem("small_prep")
        bt_done, bt_a, bt_d = sem("bt_done"), sem("bt_a"), sem("bt_d")
        gb_done, gb_a, shc_done, shf_done = sem("gb_done"), sem("gb_a"), sem("shc_done"), sem("shf_done")
        dexp_done, darg_done, dec_done, wtab_done, qw_done = sem("dexp_done"), sem("darg_done"), sem("dec_done"), sem("wtab_done"), sem("qw_done")
        st_mm, st_cp, rsc_mm, rp_done, ro_mm, ro_sq, ro_out = (sem(n) for n in (
            "st_mm", "st_cp", "rsc_mm", "rp_done", "ro_mm", "ro_sq", "ro_out"))
        sc_mm, mx_done, nm_done, ex_done, pt_mm, pt_a, pt_d, pv_mm, sk_m, sk_e, dn_done, rd_done, ya_done = (sem(n) for n in (
            "sc_mm", "mx_done", "nm_done", "ex_done", "pt_mm", "pt_a", "pt_d", "pv_mm", "sk_m", "sk_e", "dn_done", "rd_done", "ya_done"))
        mask_hi, xn2_act, nf_pool, nf_dve, root_table, fin_act = (sem(n) for n in (
            "mask_hi", "xn2_act", "nf_pool", "nf_dve", "root_table", "fin_act"))
        rr_m, rr_s, rr_r, yr_done = sem("rr_m"), sem("rr_s"), sem("rr_r"), sem("yr_done")
        yt_mm, yt_hi, yt_lo = sem("yt_mm"), sem("yt_hi"), sem("yt_lo")
        in_xr, d_scaled, d_out, d_sq = sem("in_xr"), sem("d_scaled"), sem("d_out"), sem("d_sq")
        dm_done, dsd_done, drs_done, xn2_done = sem("dm_done"), sem("dsd_done"), sem("drs_done"), sem("xn2_done")
        scc_done, gmf_done, et_mm, em_done, eh_done, el_done = (sem(n) for n in (
            "scc_done", "gmf_done", "et_mm", "em_done", "eh_done", "el_done"))
        sg_done, act_done, at_mm, at_out = sem("sg_done"), sem("act_done"), sem("at_mm"), sem("at_out")
        acc_zero2, acc_bias2, gf_mm, gf_a, gf_d = sem("acc_zero2"), sem("acc_bias2"), sem("gf_mm"), sem("gf_a"), sem("gf_d")
        sth_done, stl_done = sem("sth_done"), sem("stl_done")
        in_nf, f_scaled, f_out, f_sq, fm_done, fsd_done, frs_done, fin_done, stored = (sem(n) for n in (
            "in_nf", "f_scaled", "f_out", "f_sq", "fm_done", "fsd_done", "frs_done", "fin_done", "stored"))

        A0 = 8
        GATE_M = 0
        SHIFT_F, SCALE_F, GATE_F = D, 2 * D, D

        BT_BANKS = (2, 3, 6, 7, 5, 4, 2, 3, 6, 7)
        GB_BANKS = (2, 3, 6, 7)

        def mix_dst(g):
            if g < 4:
                return qk_t[:, g, :, :].rearrange("p a c -> p (a c)")
            if g < 8:
                return aq_t[:, 2 * (g - 4):2 * (g - 4) + 2, :].rearrange("p a c -> p (a c)")
            return ak_t[:, g - 8, :]

        def mix_evac(e, copy, g, done):
            e.wait_ge(bt_done, g + 1)
            copy(mix_dst(g), bank(BT_BANKS[g])).then_inc(done, 1)


        def xt_dst(g):
            return (xt_x if g < 8 else xt_c)[:, g % 4 * 4:g % 4 * 4 + 4, g // 4 % 2 * P:(g // 4 % 2 + 1) * P]

        def yt_slots(g):
            first = 8 + 2 * g if g < 4 else 2 * (g - 4)
            return slice(first, first + 2)

        def yt_bank(g):
            return bank(5 if g < 4 else (3, 6, 7, 5)[g - 4])

        def in_slot(k):
            return k // (KT // 2) * 2 + k % 2

        def modulate(e, k, done):
            for v, src in enumerate((xt_x, xt_c)):
                e.tensor_scalar(tmp_s[:, in_slot(k), v, :], src[:, k, :], gm[:, k // 8, k % 8, v:v + 1], modc[:, k, v:v + 1],
                                ALU.mult, ALU.add).then_inc(done, 1)

        def high_inputs(e, k, modulated, done):
            e.wait_ge(modulated, k % 8 * 2 + 2)
            e.activation(h_hi[:, k, :], tmp_s[:, in_slot(k), 0, :], ACT.Copy).then_inc(done, 1)
            e.activation(c_hi[:, k, :], tmp_s[:, in_slot(k), 1, :], ACT.Copy).then_inc(done, 1)

        def low_inputs(e, k, highs, done):
            e.wait_ge(highs, k % 8 * 2 + 2)
            for v, (h, l) in enumerate(((h_hi, h_lo), (c_hi, c_lo))):
                e.tensor_tensor(l[:, k, :], tmp_s[:, in_slot(k), v, :], h[:, k, :].bitcast(f32), ALU.subtract).then_inc(done, 1)

        block = stack.enter_context(nc.Block())

        @block.sync
        def _(sp):
            def load(n, slot, src, wait=True):
                if wait:
                    sp.wait_ge(lo_done, n - (RAW - 1))
                dst = raw[slot][:, :]
                if len(src.shape) == 3:
                    dst = dst.rearrange("p (k c) -> p k c", k=2)
                sp.dma_start(dst, src).then_inc(raw_in[slot], 16)

            def half(w, row, col):
                return w[0, ds(row, 2 * P), ds(col, CW)].rearrange("(k p) c -> p k c", p=P)

            def mod_load(m, slot, kk, col, slots=2):
                sp.wait_ge(acc_step, m * 2 + (A0 + 2 - 2 * slots))
                sp.dma_start(mraw[slot].rearrange("p (k c) -> p k c", k=2),
                             half(w_mod, kk * 2 * P, 2 * D + col)).then_inc(mraw_in[slot], 16)

            def mod_tile(q, k):
                return w_mod[0, k * P:(k + 1) * P, ds(q * 1024, 1024)]

            sp.dma_start(rows_b[0:KT, :], c.rearrange("b (k p) -> (b k) p", p=P)).then_inc(in_rows, 16)
            sp.dma_start(rows_b[KT:2 * KT, :], c_ctx.rearrange("(k p) -> k p", p=P)).then_inc(in_rows, 16)
            sp.dma_start(ca[:, :], const_a).then_inc(in_ca, 16)
            sp.dma_start(rows_a[0:96, :], b_mod.rearrange("b (k p) -> (b k) p", p=P)).then_inc(in_rows, 16)
            sp.dma_start(rows_a[96:112, :], norm_mix.rearrange("b (k p) -> (b k) p", p=P)).then_inc(in_rows, 16)
            sp.dma_start(rows_a[112:128, :], norm_ffn.rearrange("b (k p) -> (b k) p", p=P)).then_inc(in_rows, 16)
            for t in range(4):
                src = (x if t < 2 else ctx)[0, t % 2 * P:(t % 2 + 1) * P, :]
                sp.dma_start(xin[:, t, :], src).then_inc(in_x[t], 16)
            for n in range(KT):
                load(n, n % RAW, mod_tile(0, n), wait=n >= RAW)
            with sp.Fori(1, 4) as q:
                for t in range(KT):
                    load(q * KT + t, t % RAW, mod_tile(q, t))

            for t in range(CT):
                load(N_IN + t, t, half(w_in, 2 * t * P, CW))
            sp.dma_start(cb[:, :], const_b).then_inc(in_cb, 16)
            sp.wait_ge(hl_pool, KT)
            sp.wait_ge(hl_done, KT)
            with sp.Fori(0, 2) as i:
                for j, col in ((0, (i * 6 + 2) * CW), (1, (i * -3 + 3) * CW)):
                    for t in range(CT):
                        load(i * 16 + (N_IN + CT * (j + 1) + t), t, half(w_in, 2 * t * P, col))
                        for u in (2 * t, 2 * t + 1):
                            mod_load(i * 32 + (16 * j + u), u % 4, u % 8, i * (4 * CW) + (2 * j + u // 8) * CW, slots=4)
            for j, col in enumerate((6, 7, 4, 5, None)):
                for t in range(CT):
                    n = N_IN + CT * (5 + j) + t
                    if col is None:
                        load(n, t, half(w_out, 2 * t * P, 0))
                    else:
                        load(n, t, half(w_in, 2 * t * P, col * CW))
                    if j < 4 and t % 2 == 0:
                        m = 64 + 4 * j + t // 2
                        mod_load(m, m % 2, m % 8, m // 8 * CW)

            sp.wait_ge(pv_mm, 32)
            sp.wait_ge(ro_mm, RH)
            sp.dma_start(xr[:, :, :], x[0].rearrange("(t p) d -> p t d", p=P)).then_inc(in_xr, 16)
            for j in range(4):
                for t in range(CT):
                    n = N_OUT + CT * (j + 1) + t
                    if j < 3:
                        load(n, t, half(w_out, 2 * t * P, (j + 1) * CW))
                    else:
                        load(n, t, half(w_gate, 2 * t * P, 0))
                    if t % 2 == 0:
                        m = 80 + 4 * j + t // 2
                        mod_load(m, m % 2, m % 8, m // 8 * CW)

            def ffn_up(i, mods, last=False):
                for t in range(CT):
                    load(i * 16 + (N_GU + CT + t), t, half(w_up, 2 * t * P, i * CW))
                    if mods and t % 2 == 0:
                        u = t // 2
                        mod_load(i * 4 + (96 - 4 + u), u % 2, i - 1, 3 * D + u * CW)
                for t in range(CT):
                    if last:
                        load(N_DN + t, t, half(w_down, t % 2 * 2 * P, t // 2 * CW))
                    else:
                        load(i * 16 + (N_GU + 2 * CT + t), t, half(w_gate, 2 * t * P, i * CW + CW))

            ffn_up(0, False)
            sp.wait_ge(acc_bias2, 16)
            with sp.Fori(1, 9) as i:
                ffn_up(i, True)
            ffn_up(9, False)
            ffn_up(10, False, last=True)

            with sp.Fori(1, FG) as g:
                for t in range(CT):
                    load(g * CT + (N_DN + t), t, half(w_down, g * (4 * P) + t % 2 * 2 * P, t // 2 * CW))
            o = out[0].rearrange("(t p) d -> p t d", p=P)
            for t in range(TT):
                sp.wait_ge(fin_done, t + 1)
                sp.dma_start(o[:, t, :], xr[:, t, :]).then_inc(stored, 16)
            sp.wait_ge(stored, 16 * TT)

        @block.gpsimd
        def _(pool):
            steps = [0]

            def step(ins):
                steps[0] += 1
                ins.then_inc(pool_step, 1)

            def settle():
                pool.wait_ge(pool_step, steps[0])

            for r in range(A0):
                part = slice(r * 2 * D // A0, (r + 1) * 2 * D // A0)
                pool.memset(acc[:, part], 0.0).then_inc(acc_step, 1)
            pool.wait_ge(acc_step, A0)
            pool.dma_start(acc[0:1, 0:2 * D], b_mod[:, 2 * D:4 * D]).then_inc(acc_bias, 16)
            pool.wait_ge(lg_done, 1)
            step(pool.tensor_scalar(lg_n[:, :, :], lg_e[:, :, :], -1.0, None, ALU.mult))
            pool.wait_ge(in_small, 32)
            pool.tensor_scalar(nsink[:, :], sink[:, :], -1.0, None, ALU.mult).then_inc(small_prep, 1)
            settle()
            pairs = lg_n[:, :, :].rearrange("p d (h e) -> p d h e", e=2)
            for e in range(2):
                q = slice(64 * e, 64 * e + 64)
                pool.wait_ge(small_prep, 1 + e)
                pool.tensor_copy(lg_p[q, :, :], pairs[q, :, :, e]).then_inc(small_prep, 1)
            pool.wait_ge(small_prep, 3)
            pool.wait_ge(in_ca, 16)
            for lt in range(TT):
                for d in range(2):
                    pool.tensor_scalar(wexp[:, lt, d, :], lg_n[:, d, :], A("expo", 2 * lt + d, 2 * lt + d + 1), None,
                                       ALU.mult).then_inc(wexp_done, 1)

            pool.wait_ge(xt_a, 8)
            pool.wait_ge(xt_d, 8)
            pool.wait_ge(gm_done, 1)
            modulate(pool, 0, hm_pool)
            for k in range(KT // 2):
                if k + 1 < KT // 2:
                    if k:
                        pool.wait_ge(hl_pool, 2 * k)
                    modulate(pool, k + 1, hm_pool)
                low_inputs(pool, k, hh_pool, hl_pool)
            pool.wait_ge(cols_done, 4)
            pool.memset(acc[:, 2 * D:3 * D], 0.0).then_inc(acc_zero_s, 1)
            pool.wait_ge(acc_zero_s, 1)
            pool.dma_start(acc[0:1, 2 * D:3 * D], b_mod[:, 4 * D:5 * D]).then_inc(acc_bias_s, 16)

            turned = [0]

            def rope(v, cos, sin):
                for t in range(TT):
                    (a, b), cs, sn = v(t), cos(t), sin(t)
                    size = 1
                    for n in a.shape[1:]:
                        size *= n
                    tm = [rope_t[:, r, 0:size] for r in range(4)]
                    if len(a.shape) == 4:
                        tm = [r.rearrange("p (h a c) -> p h a c", a=a.shape[2], c=a.shape[3]) for r in tm]
                    else:
                        tm = [r.rearrange("p (h c) -> p h c", c=a.shape[2]) for r in tm]
                    step(pool.tensor_tensor(tm[0], a, cs, ALU.mult))
                    step(pool.tensor_tensor(tm[1], b, sn, ALU.mult))
                    step(pool.tensor_tensor(tm[2], a, sn, ALU.mult))
                    step(pool.tensor_tensor(tm[3], b, cs, ALU.mult))
                    settle()
                    pool.tensor_tensor(a, tm[0], tm[1], ALU.subtract).then_inc(rope_done, 1)
                    pool.tensor_tensor(b, tm[2], tm[3], ALU.add).then_inc(rope_done, 1)
                    turned[0] += 2
                    pool.wait_ge(rope_done, turned[0])

            def ret_half(src):
                def v(t):
                    w = src(t).rearrange("p (h c) -> p h c", c=RDK)
                    return w[:, :, 0:32], w[:, :, 32:64]
                return v

            def ax_half(src):
                def v(t):
                    w = src(t).rearrange("p (h a c) -> p h a c", a=2, c=32)
                    return w[:, :, :, 0:16], w[:, :, :, 16:32]
                return v

            def ret_tab(name):
                return lambda t: spread(A(name, 32 * t, 32 * t + 32), 1, RH)

            def ax_tab(name, heads):
                return lambda t: spread(A(name, 32 * t, 32 * t + 32).rearrange("p (a c) -> p a c", a=2), 1, heads)

            pool.wait_ge(proj_out, 5)
            rope(ret_half(lambda t: proj_x[:, 0, t, :]), ret_tab("rk_cos"), ret_tab("rk_sin"))
            pool.wait_ge(wck_done, 1)
            for lt in range(TT):
                for d in range(2):
                    pool.tensor_tensor(ckw[:, lt, d, :, :], proj_c[:, 0, lt, :].rearrange("p (h c) -> p h c", c=RDK),
                                       spread(wck[:, lt, d, :], 2, RDK), ALU.mult).then_inc(ckw_done, 1)
            rope(ax_half(lambda t: proj_x[:, 3, t, 0:256]), ax_tab("ax_cos", KVH), ax_tab("ax_sin", KVH))
            pool.wait_ge(proj_out, 6)
            rope(ret_half(lambda t: proj_y[:, 0, t, :]), ret_tab("rq_cos"), ret_tab("rq_sin"))
            for s in (1, 2):
                pool.wait_ge(proj_out, 6 + s)
                rope(ax_half(lambda t, s=s: proj_y[:, s, t, :]), ax_tab("ax_cos", 8), ax_tab("ax_sin", 8))
            pool.wait_ge(acc_step, A0 + 2 * 80)
            pool.wait_ge(in_cb, 16)
            for h in range(RH):
                if h >= 2:
                    pool.wait_ge(darg_done, h - 1)
                pool.tensor_scalar(dexp[h % 2][:, :], Bc("behind"), lg_n[:, 1, h:h + 1], None, ALU.mult).then_inc(dexp_done, 1)
            pool.wait_ge(shf_done, 4)
            pool.memset(acc[:, GATE_F:GATE_F + D], 0.0).then_inc(acc_zero2, 1)
            pool.wait_ge(acc_zero2, 1)
            pool.dma_start(acc[0:1, GATE_F:GATE_F + D], b_mod[:, 5 * D:6 * D]).then_inc(acc_bias2, 16)

        @block.scalar
        def _(act_e):
            e = act_e

            def hi(t, landed, freed):
                e.wait_ge(raw_in[t % RAW], landed)
                if freed is not None:
                    e.wait_ge(used, freed)
                e.activation(w_hi[t % SPLIT][:, :], raw[t % RAW][:, :], ACT.Copy).then_inc(hi_done, 1)

            def his(first, i, per, count):
                for t in range(LEAD, LEAD + count):
                    hi(t, i * (16 * per // RAW) + ((first + t) // RAW + 1) * 16, i * per + (first + t - (SPLIT - 1)))

            e.dma_start(lg_raw[:, :, :].rearrange("p d h -> p (d h)"),
                        ret_decay.rearrange("b d h -> b (d h)")[0].partition_broadcast(P)).then_inc(in_small, 16)
            e.dma_start(sink[:, :], attn_sink[0].partition_broadcast(P)).then_inc(in_small, 16)

            e.wait_ge(in_ca, 16)
            e.wait_ge(vec_tr, 2)
            e.activation(s32[:, :], bank(3, 0, 2 * KT), ACT.Silu).then_inc(silu_c, 1)
            e.wait_ge(silu_c, 1)
            e.activation(c4[:, :, :, 0], s32[:, :].rearrange("p (v k) -> p k v", v=2), ACT.Copy).then_inc(c4_hi, 1)

            def inputs_out(t):
                for g in (4 * t, 4 * t + 2):
                    e.wait_ge(xt_done, g + 1)
                    e.activation(xt_dst(g), bank(4 + g % 4).rearrange("p (k c) -> p k c", k=4), ACT.Copy).then_inc(xt_a, 1)

            e.activation(ident_r[:, :], ident, ACT.Copy).then_inc(mask_hi, 1)
            e.activation(mask_r[:, :], A("mask"), ACT.Copy).then_inc(mask_hi, 1)
            for t in range(4):
                e.wait_ge(in_x[t], 16)
                if t:
                    e.wait_ge(sq_done, t)
                e.activation(junk0[:, :], xin[:, t, :], ACT.Square, accum_out=stat[:, 0, t:t + 1]).then_inc(sq_done, 1)
                e.wait_ge(ms_done, t + 1)
                e.activation(stat[:, 2, t:t + 1], stat[:, 1, t:t + 1], ACT.Sqrt).then_inc(sd_done, 1)
                if t:
                    inputs_out(t - 1)
            e.wait_ge(in_small, 32)
            e.activation(lg_e[:, :, :], lg_raw[:, :, :], ACT.Exp).then_inc(lg_done, 1)
            inputs_out(3)

            e.sem_inc(proj_out, 1)
            e.sem_inc(at_out, 1)
            for n in range(LEAD):
                hi(n, 16, None)

            def mod_pass(q, inputs={}):
                for t in range(LEAD, LEAD + KT):
                    hi(t, q * (16 * KT // RAW) + (t // RAW + 1) * 16, q * KT + (t - (SPLIT - 1)))
                    if t == KT:
                        e.wait_ge(used, q * KT + KT)
                        e.activation(mod_rows[:, :], ps[0:4, 0:1024], ACT.Copy).then_inc(rows_done, 1)
                    if t in inputs:
                        high_inputs(e, inputs[t], hm_pool, hh_pool)

            with e.Fori(0, 3) as q:
                mod_pass(q)
            mod_pass(3, {6: 0, 8: 1, 9: 2, 11: 3, 12: 4, 14: 5, 16: 6, 18: 7})
            for k in range(KT // 2, KT):
                high_inputs(e, k, hm_done, hh_done)

            with e.Fori(0, 2) as i:
                for j in range(2):
                    his(N_IN + CT * j, i, 2 * CT, CT)
                    e.wait_ge(used, i * 16 + (N_IN + CT * (j + 1)))
                    if j:
                        e.wait_ge(acc_step, i * 64 + (A0 + 64))
                    e.activation(proj_x[:, ds(i * 2 + j, 1), :, :].rearrange("p s t c -> p (s t c)"),
                                 ps[:, j * 2048:j * 2048 + 1024], ACT.Copy)
                    e.activation(proj_c[:, ds(i * 2 + j, 1), :, :].rearrange("p s t c -> p (s t c)"),
                                 ps[:, j * 2048 + 1024:j * 2048 + 2048], ACT.Copy).then_inc(proj_out, 1)
            for s in range(5):
                his(N_IN + CT * (4 + s), 0, 0, CT if s < 4 else CT - 1)
                if s == 0:
                    e.wait_ge(wexp_done, 4)
                    e.activation(wck[:, :, :, :], wexp[:, :, :, :], ACT.Exp).then_inc(wck_done, 1)
                e.wait_ge(used, N_IN + CT * (5 + s))
                src = ps[:, s % 2 * 2048:s % 2 * 2048 + 1024]
                if s in (1, 2):
                    for t in range(TT):
                        ins = e.activation(proj_y[:, s, t, :].rearrange("p (h g c) -> p g h c", h=4, g=2),
                                           src[:, t * CW:(t + 1) * CW].rearrange("p (g h c) -> p g h c", g=2, h=4), ACT.Copy)
                else:
                    ins = e.activation(proj_y[:, s, :, :].rearrange("p t c -> p (t c)"), src, ACT.Silu if s >= 3 else ACT.Copy)
                ins.then_inc(proj_out, 1)
                if s == 0:
                    for n in (0, 1):
                        e.wait_ge(gb_done, n + 1)
                        e.activation(acc[:, GATE_M + n * CW:GATE_M + (n + 1) * CW], bank(GB_BANKS[n]), ACT.Copy).then_inc(gb_a, 1)

            def turned(g):
                mix_evac(e, lambda dst, src: e.activation(dst, src, ACT.Copy), g, bt_a)


            def decay(h):
                e.wait_ge(darg_done, h + 1)
                if h >= 2:
                    e.wait_ge(rp_done, h - 1)
                e.activation(dec[h % 2][:, :], darg[h % 2][:, :], ACT.Exp).then_inc(dec_done, 1)

            def weights(p):
                if p >= 2:
                    e.wait_ge(qw_done, p - 1)
                for d, name in enumerate(("pos_f", "pos_b")):
                    ins = e.activation(wtab[p % 2][:, d, :], Bc(name), ACT.Exp, scale=lg_p[:, d, p:p + 1])
                ins.then_inc(wtab_done, 1)

            def states(p):
                e.wait_ge(st_mm, p + 1)
                if p >= 2:
                    e.wait_ge(ro_mm, 2 * (p - 1))
                e.activation(s_sb[p % 2][:, :, :].rearrange("p d c -> p (d c)"), bank(0, 0, 256), ACT.Copy).then_inc(st_cp, 1)

            def probabilities(u):
                e.wait_ge(nm_done, u + 1)
                if u >= 3:
                    e.wait_ge(pt_mm, u - 2)
                e.activation(prob[u % 3][:, :], bank((3, 6, 7)[u % 3]), ACT.Exp, bias=nmax[:, u:u + 1], scale=SCALE,
                             accum_out=rsum[:, u:u + 1]).then_inc(ex_done, 1)

            e.wait_ge(small_prep, 3)
            e.wait_ge(in_cb, 16)
            turned(0)
            turned(2)
            e.wait_ge(bt_done, 4)
            decay(0)
            weights(0)
            turned(4)
            e.wait_ge(rope_done, 20)
            states(0)
            turned(6)
            turned(8)
            hi(LEAD + CT - 1, (N_OUT + LEAD - 1) // RAW * 16 + 16, N_OUT)
            for h in range(RH):
                if h + 1 < RH:
                    decay(h + 1)
                if h % 2 == 1 and h + 1 < RH:
                    weights((h + 1) // 2)
                    states((h + 1) // 2)
                e.wait_ge(ro_mm, h + 1)
                for t in range(TT):
                    if 2 * h + t >= 2:
                        e.wait_ge(ro_sq, 2 * h + t - 1)
                    e.activation(junk1[:, t, :], bank((5, 2)[h % 2], t * RDV, (t + 1) * RDV), ACT.Square,
                                 accum_out=rss[:, 0, 2 * h + t:2 * h + t + 1]).then_inc(ro_sq, 1)
                if h >= RH - 3:
                    probabilities(h - (RH - 3))

            def pt_out(u):
                e.wait_ge(pt_mm, u + 1)
                e.activation(pt[u % 2][:, :, :].rearrange("p b c -> p (b c)"), bank((1, 4)[u % 2]), ACT.Copy).then_inc(pt_a, 1)

            def output_high(g):
                e.wait_ge(yt_mm, g + 1)
                e.activation(h_hi[:, yt_slots(g), :].rearrange("p k c -> p (k c)"), yt_bank(g), ACT.Copy).then_inc(yt_hi, 1)

            for u in range(32 + 2):
                if u < 32:
                    if u >= 3:
                        probabilities(u)
                    if u == 4:
                        e.wait_ge(rr_m, 1)
                        e.activation(rss[:, 2, :], rss[:, 1, :], ACT.Sqrt).then_inc(rr_s, 1)
                    if u >= 15 and (u - 15) % 4 == 0 and u < 31:
                        output_high((u - 15) // 4)
                    if u % 8 == 7:
                        g = u // 8
                        e.wait_ge(sk_m, g + 1)
                        e.activation(sinke[:, 8 * g:8 * g + 8], sinkm[:, 8 * g:8 * g + 8], ACT.Exp).then_inc(sk_e, 1)
                if u >= 2 and (u - 2) % 2:
                    if u - 2 >= 2:
                        e.wait_ge(pv_mm, u - 3)
                    pt_out(u - 2)
            for g in range(4, 8):
                output_high(g)

            with e.Fori(0, 2) as i:
                for j in range(2):
                    his(N_OUT + CT * j, i, 2 * CT, CT)
                    e.wait_ge(d_out, i * 2 + (j + 1))
                    for t in range(TT):
                        e.activation(junk2[:, t, :], xr[:, t, ds(i * (2 * CW) + j * CW, CW)], ACT.Square,
                                     accum_out=ss_d[:, t, ds(i * 2 + j, 1)]).then_inc(d_sq, 1)
                    e.wait_ge(d_sq, i * 4 + (2 * j + 2))
            e.wait_ge(dm_done, 2)
            e.activation(st_d[:, 2, :], st_d[:, 1, :], ACT.Sqrt).then_inc(dsd_done, 1)
            for g in range(8):
                for j in range(2):
                    k = 2 * g + j
                    e.wait_ge(em_done, k + 1)
                    e.activation(h_hi[:, k, :], tmp_e[:, k % 4, :], ACT.Copy).then_inc(eh_done, 1)

            def ffn_up(i, first=False):
                his(N_GU, i, 2 * CT, CT)
                e.wait_ge(used, i * 16 + (N_GU + CT))
                if not first:
                    e.wait_ge(act_done, i)
                e.activation(sg[:, :, :].rearrange("p t c -> p (t c)"), ps[:, 0:1024], ACT.Silu).then_inc(sg_done, 1)
                if not first:
                    act_out(i - 1)
                his(N_GU + CT, i, 2 * CT, CT)

            def act_out(i):
                e.wait_ge(at_mm, i + 1)
                for t in range(TT):
                    ins = e.activation(act_t[:, ds(i * 4, 4), t * P:(t + 1) * P], bank(2 + t).rearrange("p (k c) -> p k c", k=4), ACT.Copy)
                ins.then_inc(at_out, 1)

            ffn_up(0, first=True)
            with e.Fori(1, FG) as i:
                ffn_up(i)
            act_out(FG - 1)

            def stage(g, slot):
                e.wait_ge(used, g * CT + (N_DN - CT))
                e.activation(st_hi[slot][:, :, :].rearrange("p k c -> p (k c)"),
                             act_t[:, ds(g * 4, 4), :].rearrange("p k c -> p (k c)"), ACT.Copy).then_inc(sth_done, 1)

            for n in (0, 1):
                e.wait_ge(gf_mm, n + 1)
                e.activation(acc[:, GATE_F + n * CW:GATE_F + (n + 1) * CW], bank((6, 7, 0, 1)[n]), ACT.Copy).then_inc(gf_a, 1)
            e.wait_ge(at_out, FG + 1)
            stage(0, 0)
            stage(1, 1)
            e.dma_start(nf[:, :], norm_final.partition_broadcast(P)).then_inc(in_nf, 16)
            his(N_DN, 0, 0, CT)
            stage(2, 0)
            with e.Fori(0, 4) as i:
                for j in range(2):
                    his(N_DN + CT * (1 + j), i, 2 * CT, CT)
                    stage(i * 2 + (3 + j), (1 + j) % 2)
            his(N_DN + CT * 9, 0, 0, CT)
            his(N_DN + CT * 10, 0, 0, CT - LEAD)
            for n in range(4):
                for t in range(TT):
                    e.wait_ge(f_out, n + 1)
                    if 2 * n + t:
                        e.wait_ge(f_sq, 2 * n + t)
                    e.activation(junk3[:, :], xr[:, t, n * CW:(n + 1) * CW], ACT.Square, accum_out=ss_f[:, t, n:n + 1]).then_inc(f_sq, 1)
            e.wait_ge(fm_done, 2)
            e.activation(st_f[:, 2, :], st_f[:, 1, :], ACT.Sqrt).then_inc(fsd_done, 1)

        @block.vector
        def _(e):
            def lo(t, n):
                e.wait_ge(hi_done, n + 1)
                e.tensor_tensor(w_lo[t % SPLIT][:, :], raw[t % RAW][:, :], w_hi[t % SPLIT][:, :].bitcast(f32),
                                ALU.subtract).then_inc(lo_done, 1)

            def mod_sum(i, per, first, k, col, slots=2):
                slot = first % slots
                e.wait_ge(mraw_in[slot], i * (16 // slots * per) + (first // slots + 1 - (16 if slots == 2 else 0)) * 16)
                for kl in range(2):
                    e.wait_ge(acc_step, i * (2 * per) + (A0 + 2 * first + kl))
                    a = acc[:, ds(col, CW)]
                    e.scalar_tensor_tensor(a, mraw[slot][:, kl * CW:(kl + 1) * CW], s32[:, ds(k + kl, 1)], a,
                                           ALU.mult, ALU.add).then_inc(acc_step, 1)

            e.wait_ge(vec_tr, 2)
            e.tensor_copy(vec_t[:, :], bank(2, 0, P)).then_inc(vec_cp, 1)
            e.wait_ge(c4_hi, 1)
            e.tensor_tensor(c4[:, :, :, 1], s32[:, :].rearrange("p (v k) -> p k v", v=2), c4[:, :, :, 0].bitcast(f32),
                            ALU.subtract).then_inc(c4_lo, 1)

            def inputs_out(t):
                for g in (4 * t + 1, 4 * t + 3):
                    e.wait_ge(xt_done, g + 1)
                    e.tensor_copy(xt_dst(g), bank(4 + g % 4).rearrange("p (k c) -> p k c", k=4)).then_inc(xt_d, 1)

            for t in range(4):
                e.wait_ge(sq_done, t + 1)
                e.tensor_scalar(stat[:, 1, t:t + 1], stat[:, 0, t:t + 1], 1.0 / D, EPS, ALU.mult, ALU.add).then_inc(ms_done, 1)
                e.wait_ge(sd_done, t + 1)
                e.reciprocal(stat[:, 3, t:t + 1], stat[:, 2, t:t + 1]).then_inc(rs_done, 1)
                e.wait_ge(rs_done, t + 1)
                e.tensor_scalar(xin[:, t, :], xin[:, t, :], stat[:, 3, t:t + 1], None, ALU.mult).then_inc(xn_done, 1)
                if t:
                    inputs_out(t - 1)
            inputs_out(3)
            for n in range(LEAD):
                lo(n, n)

            def mod_pass(q):
                for t in range(LEAD, LEAD + KT):
                    lo(t, q * KT + t)
                e.wait_ge(cols_done, q + 1)
                e.tensor_tensor(modc[:, ds(q * 8, 8), :], ps[:, ds(q * CW + 4 * CW, 16)].rearrange("p (b v) -> p b v", v=2),
                                spread(vec_t[:, ds(q * 8, 8)], 2, 2), ALU.add).then_inc(modc_done, 1)

            def gain(q):
                e.wait_ge(modc_done, q + 1)
                e.scalar_tensor_tensor(gm[:, q - 2, :, :], modc[:, q * 8:q * 8 + 8, :], 1.0,
                                       spread(vec_t[:, 80 + q * 8:88 + q * 8], 2, 2), ALU.add, ALU.mult).then_inc(gm_done, 1)

            with e.Fori(0, 3) as q:
                mod_pass(q)
            gain(2)
            mod_pass(3)
            gain(3)
            e.wait_ge(gm_done, 2)
            modulate(e, KT // 2, hm_done)
            for k in range(KT // 2, KT):
                if k + 1 < KT:
                    if k > KT // 2:
                        e.wait_ge(hl_done, 2 * (k - KT // 2))
                    modulate(e, k + 1, hm_done)
                low_inputs(e, k, hh_done, hl_done)

            e.wait_ge(acc_bias, 16)
            with e.Fori(0, 2) as i:
                for j in range(2):
                    for t in range(CT):
                        lo(LEAD + t, i * 16 + (N_IN + CT * j + LEAD + t))
                        for u in (2 * t, 2 * t + 1):
                            mod_sum(i, 32, 16 * j + u, 2 * (u % 8), i * (4 * CW) + (2 * j + u // 8) * CW, slots=4)
            for s in range(5):
                for t in range(CT if s < 4 else CT - 1):
                    lo(LEAD + t, N_IN + CT * (4 + s) + LEAD + t)
                    if (s, t) == (0, 0):
                        e.wait_ge(acc_bias_s, 16)
                    if s < 4 and t % 2 == 0:
                        m = 64 + 4 * s + t // 2
                        mod_sum(0, 0, m, 2 * (m % 8), m // 8 * CW)
                if s == 0:
                    for n in (2, 3):
                        e.wait_ge(gb_done, n + 1)
                        e.tensor_copy(acc[:, GATE_M + n * CW:GATE_M + (n + 1) * CW], bank(GB_BANKS[n])).then_inc(gb_d, 1)
                if s == 1:
                    for b in range(4):
                        e.wait_ge(shc_done, b + 1)
                        e.tensor_reduce(sh_f[:, 4 * b:4 * b + 4], bank(GB_BANKS[b]).rearrange("p (k c) -> p k c", k=4), AX.X, ALU.add).then_inc(shf_done, 1)

            def turned(g):
                mix_evac(e, lambda dst, src: e.tensor_copy(dst, src), g, bt_d)

            def exponents(h):
                e.wait_ge(dexp_done, h + 1)
                if h >= 2:
                    e.wait_ge(dec_done, h - 1)
                e.scalar_tensor_tensor(darg[h % 2][:, :], Bc("ahead"), lg_n[:, 0, h:h + 1], dexp[h % 2][:, :],
                                       ALU.mult, ALU.add).then_inc(darg_done, 1)

            e.wait_ge(in_cb, 16)
            e.wait_ge(used, N_OUT)
            exponents(0)
            turned(1)
            turned(3)

            def query_weights(p):
                e.wait_ge(wtab_done, p + 1)
                if p >= 2:
                    e.wait_ge(ro_mm, 2 * (p - 1))
                e.tensor_tensor(qw[p % 2][:, :, :], spread(qk_t[:, p, 0, :], 1, 2), wtab[p % 2][:, :, :], ALU.mult).then_inc(qw_done, 1)

            def decayed(h):
                e.wait_ge(rsc_mm, h + 1)
                e.wait_ge(dec_done, h + 1)
                if h >= 2:
                    e.wait_ge(ro_mm, h - 1)
                e.tensor_tensor(rp[h % 2][:, :, :].rearrange("p a c -> p (a c)"), bank((1, 4)[h % 2]), dec[h % 2][:, :], ALU.mult).then_inc(rp_done, 1)

            def row_max(u):
                h = 4 * (u // 8) + u % 4
                e.wait_ge(sc_mm, u + 1)
                e.tensor_reduce(rmax[:, u:u + 1], bank((3, 6, 7)[u % 3]), AX.X, ALU.max).then_inc(mx_done, 1)
                e.wait_ge(mx_done, u + 1)
                e.tensor_scalar(nmax[:, u:u + 1], rmax[:, u:u + 1], -SCALE, nsink[:, h:h + 1], ALU.mult, ALU.min).then_inc(nm_done, 1)

            turned(5)
            decayed(0)
            turned(7)
            query_weights(0)
            turned(9)
            exponents(1)
            lo(LEAD + CT - 1, N_OUT + LEAD - 1)
            for h in range(RH):
                if h + 1 < RH:
                    decayed(h + 1)
                if h + 2 < RH:
                    exponents(h + 2)
                if h % 2 == 1 and h + 1 < RH:
                    query_weights((h + 1) // 2)
                if h >= RH - 3:
                    row_max(h - (RH - 3))
                e.wait_ge(ro_sq, 2 * (h + 1))
                og = proj_y[:, 3 + h // 4, :, h % 4 * RDV:(h % 4 + 1) * RDV]
                e.tensor_tensor(og, bank((5, 2)[h % 2], 0, TT * RDV).rearrange("p (t c) -> p t c", t=TT), og, ALU.mult).then_inc(ro_out, 1)
            e.tensor_scalar(rss[:, 1, :], rss[:, 0, :], 1.0 / RDV, EPS, ALU.mult, ALU.add).then_inc(rr_m, 1)

            rs = rss[:, 3, :].rearrange("p (h t) -> p t h", t=TT)

            def retention_normed(n):
                hq, t = n // TT, n % TT
                og = proj_y[:, 3 + hq, t, :].rearrange("p (h c) -> p h c", h=4)
                e.tensor_tensor(og, og, spread(rs[:, t, 4 * hq:4 * hq + 4], 2, RDV), ALU.mult).then_inc(yr_done, 1)

            def output_low(g):
                e.wait_ge(yt_hi, g + 1)
                e.tensor_tensor(h_lo[:, yt_slots(g), :].rearrange("p k c -> p (k c)"), yt_bank(g),
                                h_hi[:, yt_slots(g), :].rearrange("p k c -> p (k c)").bitcast(f32), ALU.subtract).then_inc(yt_lo, 1)

            for u in range(32 + 3):
                if u < 32:
                    if u >= 3:
                        row_max(u)
                    if u == 7:
                        e.wait_ge(rr_s, 1)
                        e.reciprocal(rss[:, 3, :], rss[:, 2, :]).then_inc(rr_r, 1)
                    if 9 <= u < 13:
                        e.wait_ge(rr_r, 1)
                        retention_normed(u - 9)
                    if u >= 16 and u % 4 == 0:
                        output_low((u - 16) // 4)
                    if u % 8 == 7:
                        g = u // 8
                        e.wait_ge(nm_done, u + 1)
                        e.tensor_tensor(sinkm[:, 8 * g:8 * g + 8].rearrange("p (t h) -> p t h", t=TT),
                                        nmax[:, 8 * g:8 * g + 8].rearrange("p (t h) -> p t h", t=TT),
                                        spread(sink[:, 4 * g:4 * g + 4], 1, TT), ALU.add).then_inc(sk_m, 1)
                if 2 <= u < 34 and u % 2 == 0:
                    v = u - 2
                    e.wait_ge(pt_mm, v + 1)
                    if v >= 2:
                        e.wait_ge(pv_mm, v - 1)
                    e.tensor_copy(pt[v % 2][:, :, :].rearrange("p b c -> p (b c)"), bank((1, 4)[v % 2])).then_inc(pt_d, 1)
                if u >= 10 and (u - 3) % 8 == 7:
                    g = (u - 3) // 8
                    r = slice(8 * g, 8 * g + 8)
                    e.wait_ge(sk_e, g + 1)
                    e.tensor_tensor(den[:, r], rsum[:, r], sinke[:, r], ALU.add).then_inc(dn_done, 1)
                    e.wait_ge(dn_done, g + 1)
                    e.reciprocal(rden[:, r], den[:, r]).then_inc(rd_done, 1)
                    e.wait_ge(rd_done, g + 1)
                    e.wait_ge(pv_mm, 8 * g + 8)
                    e.tensor_tensor(proj_y[:, 1 + g // 2, :, g % 2 * 256:(g % 2 + 1) * 256].rearrange("p t (h c) -> p t h c", h=4),
                                    bank((0, 2)[g % 2]).rearrange("p (t h c) -> p t h c", t=TT, h=4),
                                    spread(rden[:, r].rearrange("p (t h) -> p t h", t=TT), 3, DH), ALU.mult).then_inc(ya_done, 1)
            for g in range(4, 8):
                output_low(g)

            e.wait_ge(in_xr, 16)
            e.sem_inc(d_scaled, 1)
            with e.Fori(0, 2) as i:
                for j in range(2):
                    for t in range(CT):
                        lo(LEAD + t, i * 16 + (N_OUT + CT * j + LEAD + t))
                        if t % 2 == 0:
                            mod_sum(i, 8, 80 + 4 * j + t // 2, 8 * j + t, i * CW + 10 * CW)
                    e.wait_ge(used, i * 16 + (N_OUT + CT * (j + 1)))
                    e.tensor_tensor(tmp_d[:, :, :], ps[:, j * 2048:j * 2048 + 1024].rearrange("p (t c) -> p t c", t=TT),
                                    spread(acc[:, ds(i * (2 * CW) + (GATE_M + j * CW), CW)], 1, TT), ALU.mult).then_inc(d_scaled, 1)
                    e.wait_ge(d_scaled, i * 2 + (j + 2))
                    xc = xr[:, :, ds(i * (2 * CW) + j * CW, CW)]
                    e.tensor_tensor(xc, tmp_d[:, :, :], xc, ALU.add).then_inc(d_out, 1)
                    e.wait_ge(d_out, i * 2 + (j + 1))
            e.wait_ge(scc_done, 1)
            e.scalar_tensor_tensor(gm_f[:, :], bank(0, 0, KT), 1.0, vec_t[:, 112:128], ALU.add, ALU.mult).then_inc(gmf_done, 1)
            e.wait_ge(d_sq, 8)
            e.tensor_reduce(st_d[:, 0, :], ss_d[:, :, :], AX.X, ALU.add).then_inc(dm_done, 1)
            e.wait_ge(dm_done, 1)
            e.tensor_scalar(st_d[:, 1, :], st_d[:, 0, :], 1.0 / D, EPS, ALU.mult, ALU.add).then_inc(dm_done, 1)
            e.wait_ge(dsd_done, 1)
            e.reciprocal(st_d[:, 3, :], st_d[:, 2, :]).then_inc(drs_done, 1)
            e.wait_ge(drs_done, 1)
            for t in range(TT):
                e.tensor_scalar(xn[:, t, :], xr[:, t, :], st_d[:, 3, t:t + 1], None, ALU.mult).then_inc(xn2_done, 1)
            e.wait_ge(gmf_done, 1)

            def modulated(k):
                e.wait_ge(et_mm, k // 2 + 1)
                if k >= 4:
                    e.wait_ge(el_done, k - 3)
                e.tensor_scalar(tmp_e[:, k % 4, :], bank((2, 3, 6, 7)[k // 2 % 4], k % 2 * 256, k % 2 * 256 + 256),
                                gm_f[:, k:k + 1], sh_f[:, k:k + 1], ALU.mult, ALU.add).then_inc(em_done, 1)

            modulated(0)
            modulated(1)
            for k in range(KT):
                if k % 2 == 0 and k + 2 < KT:
                    modulated(k + 2)
                    modulated(k + 3)
                e.wait_ge(eh_done, k + 1)
                e.tensor_tensor(h_lo[:, k, :], tmp_e[:, k % 4, :], h_hi[:, k, :].bitcast(f32), ALU.subtract).then_inc(el_done, 1)

            def ffn_up(i, mods, first=False):
                for j in range(2):
                    for t in range(CT):
                        lo(LEAD + t, i * 16 + (N_GU + CT * j + LEAD + t))
                        if mods and j == 0 and t % 2 == 0:
                            u = t // 2
                            mod_sum(i, 4, 92 + u, i * 2 - 2, GATE_F + u * CW)
                e.wait_ge(used, i * 16 + (N_GU + 2 * CT))
                e.wait_ge(sg_done, i + 1)
                if not first:
                    e.wait_ge(at_mm, i)
                e.tensor_tensor(act[:, :, :].rearrange("p t c -> p (t c)"), ps[:, 4 * CW:6 * CW],
                                sg[:, :, :].rearrange("p t c -> p (t c)"), ALU.mult).then_inc(act_done, 1)

            ffn_up(0, False, first=True)
            e.wait_ge(acc_bias2, 16)
            with e.Fori(1, 9) as i:
                ffn_up(i, True)
            with e.Fori(9, FG) as i:
                ffn_up(i, False)

            def stage(g, slot):
                e.wait_ge(sth_done, g + 1)
                e.tensor_tensor(st_lo[slot][:, :, :].rearrange("p k c -> p (k c)"), act_t[:, ds(g * 4, 4), :].rearrange("p k c -> p (k c)"),
                                st_hi[slot][:, :, :].rearrange("p k c -> p (k c)").bitcast(f32), ALU.subtract).then_inc(stl_done, 1)

            for n in (2, 3):
                e.wait_ge(gf_mm, n + 1)
                e.tensor_copy(acc[:, GATE_F + n * CW:GATE_F + (n + 1) * CW], bank((6, 7, 0, 1)[n])).then_inc(gf_d, 1)
            stage(0, 0)
            stage(1, 1)
            for t in range(CT):
                lo(LEAD + t, N_DN + LEAD + t)
            stage(2, 0)
            with e.Fori(0, 4) as i:
                for j in range(2):
                    for t in range(CT):
                        lo(LEAD + t, i * 16 + (N_DN + CT * (1 + j) + LEAD + t))
                    stage(i * 2 + (3 + j), (1 + j) % 2)
            for t in range(2 * CT - LEAD):
                lo(LEAD + t, N_DN + 9 * CT + LEAD + t)
            for n in range(4):
                e.wait_ge(used, N_DN + 10 * CT + 2 * n + 2)
                if n:
                    e.wait_ge(f_out, n)
                e.tensor_tensor(tmp_f[:, :, :], ps[:, n * 1024:(n + 1) * 1024].rearrange("p (t c) -> p t c", t=TT),
                                spread(acc[:, GATE_F + n * CW:GATE_F + (n + 1) * CW], 1, TT), ALU.mult).then_inc(f_scaled, 1)
                e.wait_ge(f_scaled, n + 1)
                xc = xr[:, :, n * CW:(n + 1) * CW]
                e.tensor_tensor(xc, tmp_f[:, :, :], xc, ALU.add).then_inc(f_out, 1)
            e.wait_ge(f_sq, 8)
            e.tensor_reduce(st_f[:, 0, :], ss_f[:, :, :], AX.X, ALU.add).then_inc(fm_done, 1)
            e.wait_ge(fm_done, 1)
            e.tensor_scalar(st_f[:, 1, :], st_f[:, 0, :], 1.0 / D, EPS, ALU.mult, ALU.add).then_inc(fm_done, 1)
            e.wait_ge(fsd_done, 1)
            e.reciprocal(st_f[:, 3, :], st_f[:, 2, :]).then_inc(frs_done, 1)
            e.wait_ge(frs_done, 1)
            e.wait_ge(in_nf, 16)
            for t in range(TT):
                e.scalar_tensor_tensor(xr[:, t, :], xr[:, t, :], st_f[:, 3, t:t + 1], nf[:, :], ALU.mult, ALU.mult).then_inc(fin_done, 1)

        @block.tensor
        def _(pe):
            def split_product(dst, a_hi, a_lo, w, w2, start, stop):
                pe.matmul(dst, a_hi, w, start=start, stop=False)
                pe.matmul(dst, a_hi, w2, start=False, stop=False)
                return pe.matmul(dst, a_lo, w, start=False, stop=stop)

            def chunk(i, per, first, operands, ready=None, slot=lambda k: k):
                for t in range(CT):
                    pe.wait_ge(lo_done, i * per + (first + t + 1))
                    for kl in range(2):
                        k = 2 * t + kl
                        if ready is not None:
                            pe.wait_ge(*ready(k))
                        cols = slice(kl * CW, (kl + 1) * CW)
                        for hi, lo, tok, b in operands:
                            ins = split_product(bank(b), hi[:, slot(k), tok:tok + P], lo[:, slot(k), tok:tok + P],
                                                w_hi[t % SPLIT][:, cols], w_lo[t % SPLIT][:, cols], k == 0, k == KT - 1)
                    ins.then_inc(used, 1)

            def latents(b):
                return [(h_hi, h_lo, 0, b), (h_hi, h_lo, P, b + 1)]

            pe.wait_ge(in_rows, 80)
            pe.wait_ge(in_ca, 16)
            pe.transpose(bank(3, 0, 2 * KT), rows_b[:, :], ident[0:2 * KT, 0:2 * KT]).then_inc(vec_tr, 1)
            pe.transpose(bank(2, 0, P), rows_a[:, :], ident).then_inc(vec_tr, 1)
            for g in range(16):
                pe.wait_ge(xn_done, g // 4 + 1)
                if g >= 4:
                    pe.wait_ge(xt_d if g % 2 else xt_a, (g - 4) // 2 + 1)
                for b in range(4):
                    k = g % 4 * 4 + b
                    ins = pe.transpose(bank(4 + g % 4, b * P, (b + 1) * P), xin[:, g // 4, k * P:(k + 1) * P], ident)
                ins.then_inc(xt_done, 1)
            pe.wait_ge(xt_a, 8)
            pe.wait_ge(xt_d, 8)
            pe.wait_ge(vec_cp, 1)
            pe.wait_ge(c4_lo, 1)
            with pe.Fori(0, 4) as q:
                for t in range(KT):
                    pe.wait_ge(lo_done, q * KT + (t + 1))
                    lhs = c4[:, t, :, :].rearrange("p v s -> p (v s)")
                    for b in range(2):
                        dst = bank(b)[0:4, :]
                        cols = slice(b * CW, (b + 1) * CW)
                        pe.matmul(dst, lhs, w_hi[t % SPLIT][:, cols], start=t == 0, stop=False)
                        ins = pe.matmul(dst, lhs, w_lo[t % SPLIT][:, cols], start=False, stop=t == KT - 1)
                    ins.then_inc(used, 1)
                pe.wait_ge(rows_done, q + 1)
                for b in range(8):
                    ins = pe.matmul(ps[:, ds(q * CW + (4 * CW + 2 * b), 2)], mod_rows[:, b * P:(b + 1) * P], A("sel")[0:4, :], start=True, stop=True)
                ins.then_inc(cols_done, 1)

            with pe.Fori(0, 2) as i:
                for j in range(2):
                    if j:
                        pe.wait_ge(proj_out, i * 2 + 1)
                    chunk(i, 16, N_IN + CT * j, latents(4 * j) + [(c_hi, c_lo, 0, 4 * j + 2), (c_hi, c_lo, P, 4 * j + 3)],
                          lambda k: (hl_pool, 2 * k + 2) if k < KT // 2 else (hl_done, 2 * k + 2 - KT))
                pe.wait_ge(proj_out, i * 2 + 2)
            for j in range(5):
                pe.wait_ge(proj_out, j + 4)
                chunk(0, 0, N_IN + (4 + j) * CT, latents(j % 2 * 4))
                if j == 0:
                    pe.wait_ge(acc_step, A0 + 2 * 32)
                    pe.wait_ge(proj_out, 5)
                    for n in range(4):
                        pe.matmul(bank(GB_BANKS[n]), A("ones"), acc[:, GATE_M + n * CW:GATE_M + (n + 1) * CW], start=True, stop=True).then_inc(gb_done, 1)
                if j == 1:
                    pe.wait_ge(acc_step, A0 + 2 * 64)
                    pe.wait_ge(gb_a, 2)
                    pe.wait_ge(gb_d, 2)
                    for b in range(KT):
                        ins = pe.transpose(bank(GB_BANKS[b // 4], b % 4 * P, (b % 4 + 1) * P), acc[:, SHIFT_F + b * P:SHIFT_F + (b + 1) * P], ident)
                        if b % 4 == 3:
                            ins.then_inc(shc_done, 1)
            pe.wait_ge(shf_done, 4)

            def turn_group(g):
                pe.wait_ge(rope_done, 12 if g < 4 else 20)
                if g >= 6:
                    pe.wait_ge(bt_d if g % 2 else bt_a, (g - 6) // 2 + 1)
                b = BT_BANKS[g]
                for t in range(TT):
                    lohi = [(t * P, (t + 1) * P), ((2 + t) * P, (3 + t) * P)]
                    if g < 4:
                        srcs = [proj_y[:, 0, t, g * P:(g + 1) * P], proj_x[:, 0, t, g * P:(g + 1) * P]]
                    elif g < 8:
                        srcs = [proj_y[:, 1 + pr // 4, t, pr % 4 * P:(pr % 4 + 1) * P] for pr in (2 * g - 8, 2 * g - 7)]
                    else:
                        srcs = [pj[:, 3, t, (g - 8) * P:(g - 7) * P] for pj in (proj_x, proj_c)]
                    for (lo_, hi_), src in zip(lohi, srcs):
                        ins = pe.transpose(bank(b, lo_, hi_), src, ident)
                ins.then_inc(bt_done, 1)

            for g in range(4):
                turn_group(g)

            def states(p):
                if p:
                    pe.wait_ge(st_cp, p)
                for s in range(2):
                    h = 2 * p + s
                    for d in range(2):
                        for lt in range(TT):
                            ins = pe.matmul(ps[64 * s:64 * s + 64, d * RDV:(d + 1) * RDV], ckw[:, lt, d, h, :],
                                            proj_c[:, 1 + h // 4, lt, h % 4 * RDV:(h % 4 + 1) * RDV], start=lt == 0, stop=lt == TT - 1)
                ins.then_inc(st_mm, 1)

            def scores(h):
                if h >= 2:
                    pe.wait_ge(rp_done, h - 1)
                q = slice(64 * (h % 2), 64 * (h % 2) + 64)
                for jt in range(TT):
                    ins = pe.matmul(bank((1, 4)[h % 2], jt * SEQ, (jt + 1) * SEQ), qk_t[q, h // 2, 1, jt * P:(jt + 1) * P],
                                    qk_t[q, h // 2, 0, :], start=True, stop=True)
                ins.then_inc(rsc_mm, 1)

            def attention_scores(u):
                t, kv = u % 8 // 4, u // 8
                q = slice(64 * (kv % 2), 64 * (kv % 2) + 64)
                if u >= 3:
                    pe.wait_ge(ex_done, u - 2)
                b = (3, 6, 7)[u % 3]
                pe.matmul(bank(b), aq_t[q, kv // 2 * 4 + u % 4, t * P:(t + 1) * P], ak_t[q, kv // 2, :], start=True, stop=False)
                far = slice(P, 2 * P) if t == 0 else slice(0, P)
                pe.matmul(bank(b, far.start, far.stop), ident_r[:, :], mask_r[:, t * P:(t + 1) * P], start=False, stop=True).then_inc(sc_mm, 1)

            pe.wait_ge(proj_out, 10)
            pe.wait_ge(bt_a, 1)
            scores(0)
            pe.wait_ge(ckw_done, 4)
            states(0)
            for g in range(4, 10):
                turn_group(g)
            pe.wait_ge(bt_a, 3)
            pe.wait_ge(bt_d, 3)
            pe.wait_ge(mask_hi, 2)
            for h in range(RH):
                if h + 1 < RH:
                    scores(h + 1)
                if h % 2 == 1 and h + 1 < RH:
                    states((h + 1) // 2)
                if h == 1:
                    pe.wait_ge(bt_a, 5)
                    pe.wait_ge(bt_d, 5)
                if h >= RH - 3:
                    attention_scores(h - (RH - 3))
                pe.wait_ge(rp_done, h + 1)
                pe.wait_ge(qw_done, h // 2 + 1)
                pe.wait_ge(st_cp, h // 2 + 1)
                if h >= 2:
                    pe.wait_ge(ro_out, h - 1)
                q = slice(64 * (h % 2), 64 * (h % 2) + 64)
                for t in range(TT):
                    dst = bank((5, 2)[h % 2], t * RDV, (t + 1) * RDV)
                    tok = slice(t * P, (t + 1) * P)
                    for jt in range(TT):
                        pe.matmul(dst, rp[h % 2][:, jt, tok], proj_x[:, 1 + h // 4, jt, h % 4 * RDV:(h % 4 + 1) * RDV], start=jt == 0, stop=False)
                    for d in range(2):
                        ins = pe.matmul(dst, qw[h // 2 % 2][q, d, tok], s_sb[h // 2 % 2][q, d, :], start=False, stop=d == 1)
                ins.then_inc(ro_mm, 1)

            def output_turned(g):
                if g < 4:
                    pe.wait_ge(yr_done, 2 * (g // 2) + 2)
                    if g:
                        pe.wait_ge(yt_lo, g)
                else:
                    pe.wait_ge(ya_done, g - 3)
                    pe.wait_ge(yt_lo, 4)
                for kl in range(2):
                    k = 2 * (g % 4) + kl
                    s, col = (3 if g < 4 else 1) + k // 4, k % 4 * P
                    for t in range(TT):
                        ins = pe.transpose(yt_bank(g)[:, kl * 256 + t * P:kl * 256 + (t + 1) * P], proj_y[:, s, t, col:col + P], ident)
                ins.then_inc(yt_mm, 1)

            for u in range(32 + 3):
                if 3 <= u < 32:
                    attention_scores(u)
                if 14 <= u < 30 and (u - 14) % 4 == 0:
                    output_turned((u - 14) // 4)
                if 2 <= u < 34:
                    v = u - 2
                    pe.wait_ge(ex_done, v + 1)
                    if v >= 2:
                        pe.wait_ge(pt_a if v % 2 else pt_d, v // 2)
                    for kb in range(4):
                        ins = pe.transpose(bank((1, 4)[v % 2], kb * P, (kb + 1) * P), prob[v % 3][:, kb * P:(kb + 1) * P], ident)
                    ins.then_inc(pt_mm, 1)
                if u >= 3:
                    v = u - 3
                    g = v // 8
                    pe.wait_ge(pt_a if v % 2 else pt_d, v // 2 + 1)
                    if v % 8 == 0:
                        if g >= 2:
                            pe.wait_ge(ya_done, g - 1)
                        else:
                            pe.wait_ge(ro_out, RH)
                    for kb in range(4):
                        pj = proj_x if kb < 2 else proj_c
                        ins = pe.matmul(bank((0, 2)[g % 2], v % 8 * DH, (v % 8 + 1) * DH), pt[v % 2][:, kb, :],
                                        pj[:, 3, kb % 2, 256 + g * DH:256 + (g + 1) * DH], start=kb == 0, stop=kb == 3)
                    ins.then_inc(pv_mm, 1)

            pe.wait_ge(ex_done, 32)
            for g in range(4, 8):
                output_turned(g)
            with pe.Fori(0, 2) as i:
                for j in range(2):
                    if j:
                        pe.wait_ge(d_scaled, i * 2 + 1)
                    chunk(i, 16, N_OUT + CT * j, latents(4 * j), lambda k: (yt_lo, k // 2 + 1), lambda k: (k + 8) % KT)
                pe.wait_ge(d_scaled, i * 2 + 2)
            pe.wait_ge(acc_step, A0 + 2 * 96)
            for b in range(KT):
                ins = pe.matmul(bank(0, b, b + 1), acc[:, SCALE_F + b * P:SCALE_F + (b + 1) * P], A("ones", 0, 1), start=True, stop=True)
            ins.then_inc(scc_done, 1)
            pe.wait_ge(xn2_done, 2)
            for g in range(8):
                if g >= 4:
                    pe.wait_ge(em_done, 2 * (g - 3))
                for kl in range(2):
                    k = 2 * g + kl
                    for t in range(TT):
                        ins = pe.transpose(bank((2, 3, 6, 7)[g % 4], kl * 256 + t * P, kl * 256 + (t + 1) * P), xn[:, t, k * P:(k + 1) * P], ident)
                ins.then_inc(et_mm, 1)

            def turn(i):
                pe.wait_ge(act_done, i + 1)
                pe.wait_ge(at_out, i + 1)
                for t in range(TT):
                    for b in range(4):
                        ins = pe.transpose(bank(2 + t, b * P, (b + 1) * P), act[:, t, b * P:(b + 1) * P], ident)
                ins.then_inc(at_mm, 1)

            pe.wait_ge(gmf_done, 1)
            pe.wait_ge(d_scaled, 5)
            chunk(0, 0, N_GU, latents(0), lambda k: (el_done, k + 1))
            chunk(0, 0, N_GU + CT, latents(4))
            with pe.Fori(1, FG) as i:
                pe.wait_ge(sg_done, i)
                chunk(i, 16, N_GU, latents(0))
                turn(i - 1)
                chunk(i, 16, N_GU + CT, latents(4))
            turn(FG - 1)
            pe.wait_ge(acc_step, A0 + 2 * 128)
            pe.wait_ge(sg_done, FG)
            for n in range(4):
                pe.matmul(bank((6, 7, 0, 1)[n]), A("ones"), acc[:, GATE_F + n * CW:GATE_F + (n + 1) * CW], start=True, stop=True).then_inc(gf_mm, 1)

            def group(g, i, per, first, slot, start=False, stop=False):
                pe.wait_ge(stl_done, g + 1)
                for t in range(CT):
                    pe.wait_ge(lo_done, i * per + (first + t + 1))
                    for kl in range(2):
                        k = t % 2 * 2 + kl
                        cols = slice(kl * CW, (kl + 1) * CW)
                        for tt in range(TT):
                            ins = split_product(bank(t // 2 * 2 + tt), st_hi[slot][:, k, tt * P:(tt + 1) * P],
                                                st_lo[slot][:, k, tt * P:(tt + 1) * P], w_hi[t % SPLIT][:, cols],
                                                w_lo[t % SPLIT][:, cols], start and k == 0, stop and k == 3)
                    ins.then_inc(used, 1)

            pe.wait_ge(gf_a, 2)
            pe.wait_ge(gf_d, 2)
            pe.wait_ge(at_out, FG + 1)
            group(0, 0, 0, N_DN, 0, start=True)
            with pe.Fori(0, 4) as i:
                for j in range(2):
                    group(i * 2 + (1 + j), i, 16, N_DN + CT * (1 + j), (1 + j) % 2)
            group(9, 0, 0, N_DN + 9 * CT, 1)
            group(10, 0, 0, N_DN + 10 * CT, 0, stop=True)


def constants(np):
    a = np.zeros((P, NCA), np.float32)
    b = np.zeros((P, NCB), np.float32)

    def put(dst, cols, name, v):
        s, e = cols[name]
        dst[:, s:e] = np.asarray(v).reshape(P, e - s)

    p = np.arange(P)
    tok = np.arange(SEQ).reshape(TT, P)
    put(a, CA, "ident", np.eye(P))
    put(a, CA, "ones", np.ones((P, P)))
    far = np.where(p[None, :] > p[:, None], -1e30, 0.0), np.where(p[:, None] > p[None, :], -1e30, 0.0)
    put(a, CA, "mask", np.concatenate(far, 1))
    inv = np.float32(10000.0) ** (-np.arange(32, dtype=np.float32) / np.float32(32))
    ang = (tok[..., None].astype(np.float32) * inv).transpose(1, 0, 2)
    for name, scale in (("rq", RDK ** -0.5), ("rk", 1.0)):
        put(a, CA, name + "_cos", scale * np.cos(ang))
        put(a, CA, name + "_sin", scale * np.sin(ang))
    inv = np.float32(10000.0) ** (-np.arange(16, dtype=np.float32) / np.float32(16))
    pos = np.stack([tok // 64, tok % 64], -1).astype(np.float32)
    ang = (pos[..., None] * inv).transpose(1, 0, 2, 3)
    put(a, CA, "ax_cos", np.cos(ang))
    put(a, CA, "ax_sin", np.sin(ang))
    ctx = np.arange(CTX).reshape(TT, P)
    put(a, CA, "expo", np.stack([CTX - 1 - ctx, ctx], -1).transpose(1, 0, 2))
    a[0:4, CA["sel"][0]:CA["sel"][1]] = [[1, 0], [1, 0], [0, 1], [0, 1]]
    rel = np.arange(SEQ)[None, None, :] - tok.T[:, :, None]
    put(b, CB, "ahead", np.maximum(rel, 0))
    put(b, CB, "behind", np.maximum(-rel, 0))
    put(b, CB, "pos_f", np.broadcast_to(np.arange(SEQ) + 1, (P, SEQ)))
    put(b, CB, "pos_b", np.broadcast_to(SEQ - np.arange(SEQ), (P, SEQ)))
    return a, b


_INS = ["x", "c", "ctx", "c_ctx", "w_mod", "b_mod", "norm_mix", "norm_ffn", "w_in", "ret_decay", "attn_sink",
        "w_out", "w_gate", "w_up", "w_down", "norm_final"]


def kernel(**inputs):
    import numpy as np
    import concourse.bacc as bacc
    from concourse.bass_utils import run_bass_kernel_spmd

    nc = bacc.Bacc("TRN2", target_bir_lowering=False, num_devices=1)
    const_a, const_b = constants(np)
    arrays = {name: np.ascontiguousarray(inputs[name]) for name in _INS}
    arrays["const_a"], arrays["const_b"] = const_a, const_b
    args = [nc.dram_tensor(name, a.shape, mybir.dt.from_np(a.dtype), kind="ExternalInput").ap()
            for name, a in arrays.items()]
    out = nc.dram_tensor("out", (1, SEQ, D), mybir.dt.float32, kind="ExternalOutput").ap()
    build(nc, *args, out)
    r = run_bass_kernel_spmd(nc, [arrays], core_ids=[0])
    return r.results[0]["out"]
```
